# Optimizing a Trainium2 kernel written in Bass

```python
import math
import jax
import jax.numpy as jnp
from jax import lax
import numpy as np

D_MODEL = 1024
BATCH = 1
SEQ = 512
DEPTH = 1

GRID_W = 64
CTX_LEN = 256
EPS = 1e-6
F32 = jnp.float32

D_HY = 512
HY_SHORT = 3
HY_POS_BANDS = 16
HY_POS_DIM = 1 + 2 * HY_POS_BANDS
HY_FFN = 64
HY_N_FILT = 4

GLA_HEADS = 4
GLA_DK = 64
GLA_DV = 128
GLA_QK = GLA_HEADS * GLA_DK
GLA_V = GLA_HEADS * GLA_DV
GLA_LOWRANK = 16
GLA_TAU = 16.0
GLA_CHUNK = 64

S5_CH = 512
S5_GROUP = 16
S5_GROUPS = S5_CH // S5_GROUP
S5_STATE = 64

D_FF = ((8 * D_MODEL + 3 * 256 - 1) // (3 * 256)) * 256

COL_SIZES = (GLA_QK, GLA_V, 2 * GLA_LOWRANK, S5_CH, GLA_QK, GLA_V, 3 * D_HY, 3 * D_MODEL)
N_STATE_COLS = GLA_QK + GLA_V + 2 * GLA_LOWRANK + S5_CH
N_IN = N_STATE_COLS + GLA_QK + GLA_V + 3 * D_HY + 3 * D_MODEL

kernel_name = 'hybrid_hyena_gla_s5_prefix_dit'

def rmsnorm(x, g):
    xf = x.astype(F32)
    y = xf * lax.rsqrt(jnp.mean(xf * xf, axis=-1, keepdims=True) + EPS)
    return (y * g.astype(F32)).astype(x.dtype)

def modulation(cond, w_mod, b_mod, n_chunks):
    cols = n_chunks * D_MODEL
    m = jax.nn.silu(cond) @ w_mod[:, :cols] + b_mod[:cols]
    return jnp.split(m[:, None, :], n_chunks, axis=-1)

def split_cols(p, sizes):
    idx = [int(s) for s in np.cumsum(sizes)[:-1]]
    return jnp.split(p, idx, axis=-1)

def short_conv(u, w):
    K = w.shape[0]
    pad = K // 2
    L = u.shape[1]
    up = jnp.pad(u, ((0, 0), (pad, pad), (0, 0)))
    return sum(up[:, j:j + L] * w[j] for j in range(K))

def hyena_filters(L, params):
    w1, b1, w2, b2, w3, freq1, freq2, decay = (p.astype(F32) for p in params)
    t = jnp.linspace(0.0, 1.0, L, dtype=F32)[:, None]
    bands = jnp.linspace(1e-4, HY_POS_BANDS - 1, HY_POS_BANDS, dtype=F32)
    ang = (2.0 * math.pi / L) * jnp.arange(L, dtype=F32)[:, None] * bands[None]
    z = jnp.concatenate([t, jnp.cos(ang), -jnp.sin(ang)], axis=-1)
    hid = jnp.sin(freq1 * (z @ w1 + b1))
    hid = jnp.sin(freq2 * (hid @ w2 + b2))
    h = (hid @ w3) * jnp.exp(-t * jnp.abs(decay))
    return h.reshape(L, HY_N_FILT, D_HY)

def long_conv_bidir(u, h_fwd, h_bwd, bias):
    L = u.shape[1]
    k = jnp.concatenate([h_fwd[:1] + h_bwd[:1], h_fwd[1:], jnp.zeros_like(h_fwd[:1]), h_bwd[:0:-1]], axis=0)
    k = k * lax.rsqrt(jnp.sum(k * k, axis=0, keepdims=True) + EPS)
    u_f = jnp.fft.rfft(u, n=2 * L, axis=1)
    k_f = jnp.fft.rfft(k, axis=0)
    y = jnp.fft.irfft(u_f * k_f[None], n=2 * L, axis=1)[:, :L]
    return y + u * bias

def hyena_mix(cols, conv_w, filt_params, bias):
    u = short_conv(cols.astype(F32), conv_w.astype(F32))
    x1, x2, v = jnp.split(u, 3, axis=-1)
    h = hyena_filters(cols.shape[1], filt_params)
    bias = bias.astype(F32)
    z = x1 * long_conv_bidir(v, h[:, 0], h[:, 1], bias[0])
    return x2 * long_conv_bidir(z, h[:, 2], h[:, 3], bias[1])

def to_heads(t, d):
    B, L, _ = t.shape
    return t.astype(F32).reshape(B, L, GLA_HEADS, d).transpose(0, 2, 1, 3)

def gla_decays(a_lr, wa2, ba):
    B, L, _ = a_lr.shape
    z = jnp.einsum('bldr,drk->bldk', a_lr.astype(F32).reshape(B, L, 2, GLA_LOWRANK), wa2.astype(F32)) + ba.astype(F32)
    log_a = jax.nn.log_sigmoid(z) / GLA_TAU
    return to_heads(log_a[:, :, 0], GLA_DK), to_heads(log_a[:, :, 1], GLA_DK)

def gla_scan(k, v, log_a, S0, q=None):
    B, H, L, DK = k.shape
    DV = v.shape[-1]
    C = GLA_CHUNK
    N = L // C
    blk = lambda t: t.reshape(B, H, N, C, t.shape[-1])
    k, v = blk(k), blk(v)
    b = jnp.cumsum(blk(log_a), axis=3)
    b_last = b[:, :, :, -1:]
    dS = jnp.einsum('bhncd,bhnce->bhnde', k * jnp.exp(b_last - b), v)
    decay = jnp.exp(b_last[:, :, :, 0])
    want = q is not None

    def step(S, inp):
        dec, ds = inp
        return dec[..., None] * S + ds, (S if want else None)

    S_fin, S_prev = lax.scan(step, S0, (jnp.moveaxis(decay, 2, 0), jnp.moveaxis(dS, 2, 0)))
    if not want:
        return None, S_fin
    q_dec = blk(q) * jnp.exp(b)
    att = jnp.einsum('bhncd,bhnsd->bhncs', q_dec, k * jnp.exp(-b))
    att = jnp.where(jnp.tril(jnp.ones((C, C), bool)), att, 0.0)
    o = jnp.einsum('bhncs,bhnse->bhnce', att, v) + jnp.einsum('bhncd,bhnde->bhnce', q_dec, jnp.moveaxis(S_prev, 0, 2))
    return o.reshape(B, H, L, DV), S_fin

def gla_bidir(k, v, la_f, la_b, S0_f, S0_b, q=None):
    fl = lambda t: jnp.flip(t, axis=2)
    o_f, S_f = gla_scan(k, v, la_f, S0_f, q)
    o_b, S_b = gla_scan(fl(k), fl(v), fl(la_b), S0_b, None if q is None else fl(q))
    o = None if q is None else o_f + fl(o_b)
    return o, S_f, S_b

def gla_readout(o, r, gnorm):
    o = rmsnorm(o, gnorm)
    B, H, L, DV = o.shape
    return o.transpose(0, 2, 1, 3).reshape(B, L, H * DV) * jax.nn.silu(r.astype(F32))

def s5_discretize(a_re, a_im, log_dt, b_re, b_im):
    lam = lax.complex(jnp.minimum(a_re.astype(F32), -1e-4), a_im.astype(F32))
    lam_dt = lam * jnp.exp(log_dt.astype(F32))[:, None]
    b_bar = ((jnp.exp(lam_dt) - 1.0) / lam)[..., None] * lax.complex(b_re.astype(F32), b_im.astype(F32))
    return lam_dt, b_bar

def s5_scan(u, lam_dt, b_bar, x0, c_mat=None):
    Bn, L, G, I = u.shape
    T = GRID_W
    rows = L // T
    lam_bar = jnp.exp(lam_dt)
    pows = jnp.exp(lam_dt[None] * jnp.arange(1, T + 1, dtype=F32)[:, None, None])
    u_blocks = jnp.moveaxis(u.reshape(Bn, rows, T, G, I), 1, 0)

    def combine(e1, e2):
        a1, b1 = e1
        a2, b2 = e2
        return a1 * a2, a2 * b1 + b2

    def step(x, u_blk):
        bu = jnp.einsum('btgi,gpi->btgp', u_blk.astype(jnp.complex64), b_bar)
        _, xs = lax.associative_scan(combine, (jnp.broadcast_to(lam_bar, bu.shape), bu), axis=1)
        xs = xs + pows[None] * x[:, None]
        y = None if c_mat is None else jnp.einsum('btgp,gip->btgi', xs, c_mat).real
        return xs[:, -1], y

    x_fin, ys = lax.scan(step, x0, u_blocks)
    if c_mat is None:
        return None, x_fin
    return jnp.moveaxis(ys, 0, 1).reshape(Bn, L, G, I), x_fin

def s5_bidir(u, disc_f, disc_b, x0_f, x0_b, c_mat=None):
    y_f, x_f = s5_scan(u, disc_f[0], disc_f[1], x0_f, c_mat)
    y_b, x_b = s5_scan(jnp.flip(u, 1), disc_b[0], disc_b[1], x0_b, c_mat)
    y = None if c_mat is None else y_f + jnp.flip(y_b, 1)
    return y, x_f, x_b

def to_groups(u):
    B, L, _ = u.shape
    return u.astype(F32).reshape(B, L, S5_GROUPS, S5_GROUP)

def s5_readout(y, u, d, w_glu, b_glu):
    B, L, _ = u.shape
    y = y.reshape(B, L, S5_CH) + d.astype(F32) * u.astype(F32)
    g = jax.nn.gelu(y)
    return g * jax.nn.sigmoid(g @ w_glu.astype(F32) + b_glu.astype(F32))

def merge_branches(y_hy, y_gla, y_s5, gates, w_hy, w_gla, w_s5, w_out):
    g_hy, g_gla, g_s5 = jnp.split(gates.astype(F32), 3, axis=-1)
    m = (jax.nn.sigmoid(g_hy) * (y_hy @ w_hy.astype(F32))
         + jax.nn.sigmoid(g_gla) * (y_gla @ w_gla.astype(F32))
         + jax.nn.sigmoid(g_s5) * (y_s5 @ w_s5.astype(F32)))
    return m @ w_out.astype(F32)

def swiglu(h, w_in, w_out):
    a, b = jnp.split(h @ w_in, 2, axis=-1)
    return (jax.nn.silu(a) * b) @ w_out

def setup_inputs(seed: int = 0) -> dict:
    key = jax.random.key(seed)
    ks = iter(jax.random.split(key, 48))
    nrm = lambda shape, scale: scale * jax.random.normal(next(ks), shape, F32)
    G, P, I = S5_GROUPS, S5_STATE, S5_GROUP
    n_idx = jnp.arange(P, dtype=F32)
    decay_init = jnp.linspace(math.log(1e-2) / 0.3, math.log(1e-2) / 1.5, HY_N_FILT * D_HY, dtype=F32)
    return {
        'x': nrm((BATCH, SEQ, D_MODEL), 1.0),
        'c': nrm((BATCH, D_MODEL), 1.0),
        'ctx': nrm((BATCH, CTX_LEN, D_MODEL), 1.0),
        'c_ctx': nrm((D_MODEL,), 1.0),
        'w_mod': nrm((DEPTH, D_MODEL, 6 * D_MODEL), 0.5 * D_MODEL ** -0.5),
        'b_mod': nrm((DEPTH, 6 * D_MODEL), 0.02),
        'g_norm1': 1.0 + nrm((DEPTH, D_MODEL), 0.02),
        'g_norm2': 1.0 + nrm((DEPTH, D_MODEL), 0.02),
        'w_in': nrm((DEPTH, D_MODEL, N_IN), D_MODEL ** -0.5),
        'hy_conv': nrm((DEPTH, HY_SHORT, 3 * D_HY), HY_SHORT ** -0.5),
        'hy_w1': nrm((DEPTH, HY_POS_DIM, HY_FFN), HY_POS_DIM ** -0.5),
        'hy_b1': nrm((DEPTH, HY_FFN), 0.02),
        'hy_w2': nrm((DEPTH, HY_FFN, HY_FFN), HY_FFN ** -0.5),
        'hy_b2': nrm((DEPTH, HY_FFN), 0.02),
        'hy_w3': nrm((DEPTH, HY_FFN, HY_N_FILT * D_HY), HY_FFN ** -0.5),
        'hy_freq1': 1.0 + nrm((DEPTH, HY_FFN), 0.02),
        'hy_freq2': 1.0 + nrm((DEPTH, HY_FFN), 0.02),
        'hy_decay': decay_init + nrm((DEPTH, HY_N_FILT * D_HY), 0.1),
        'hy_bias': nrm((DEPTH, 2, D_HY), 0.3),
        'gla_wa2': nrm((DEPTH, 2, GLA_LOWRANK, GLA_QK), GLA_LOWRANK ** -0.5),
        'gla_ba': nrm((DEPTH, 2, GLA_QK), 0.02),
        'gla_gnorm': 1.0 + nrm((DEPTH, GLA_DV), 0.02),
        's5_a_re': -0.5 + nrm((DEPTH, 2, G, P), 0.01),
        's5_a_im': math.pi * n_idx + nrm((DEPTH, 2, G, P), 0.01),
        's5_log_dt': jax.random.uniform(next(ks), (DEPTH, 2, G), F32, math.log(1e-3), math.log(1e-1)),
        's5_b_re': nrm((DEPTH, G, P, I), (2 * I) ** -0.5),
        's5_b_im': nrm((DEPTH, G, P, I), (2 * I) ** -0.5),
        's5_c_re': nrm((DEPTH, G, I, P), P ** -0.5),
        's5_c_im': nrm((DEPTH, G, I, P), P ** -0.5),
        's5_d': nrm((DEPTH, S5_CH), 0.5),
        's5_w_glu': nrm((DEPTH, S5_CH, S5_CH), S5_CH ** -0.5),
        's5_b_glu': nrm((DEPTH, S5_CH), 0.02),
        'w_br_hy': nrm((DEPTH, D_HY, D_MODEL), D_HY ** -0.5),
        'w_br_gla': nrm((DEPTH, GLA_V, D_MODEL), GLA_V ** -0.5),
        'w_br_s5': nrm((DEPTH, S5_CH, D_MODEL), S5_CH ** -0.5),
        'w_out': nrm((DEPTH, D_MODEL, D_MODEL), D_MODEL ** -0.5),
        'w_ffn_in': nrm((DEPTH, D_MODEL, 2 * D_FF), D_MODEL ** -0.5),
        'w_ffn_out': nrm((DEPTH, D_FF, D_MODEL), D_FF ** -0.5),
        'g_final': 1.0 + nrm((D_MODEL,), 0.02),
    }

def reference(x, c, ctx, c_ctx, w_mod, b_mod, g_norm1, g_norm2, w_in, hy_conv, hy_w1, hy_b1, hy_w2, hy_b2,
              hy_w3, hy_freq1, hy_freq2, hy_decay, hy_bias, gla_wa2, gla_ba, gla_gnorm, s5_a_re, s5_a_im,
              s5_log_dt, s5_b_re, s5_b_im, s5_c_re, s5_c_im, s5_d, s5_w_glu, s5_b_glu, w_br_hy, w_br_gla,
              w_br_s5, w_out, w_ffn_in, w_ffn_out, g_final):
    Bn = x.shape[0]
    zeros_S = jnp.zeros((Bn, GLA_HEADS, GLA_DK, GLA_DV), F32)
    zeros_x = jnp.zeros((Bn, S5_GROUPS, S5_STATE), jnp.complex64)
    q_scale = GLA_DK ** -0.5
    for l in range(DEPTH):
        last = l == DEPTH - 1
        sh1, sc1, gt1, sh2, sc2, gt2 = modulation(c, w_mod[l], b_mod[l], 6)
        mods_c = modulation(c_ctx[None], w_mod[l], b_mod[l], 2 if last else 6)
        h = rmsnorm(x, g_norm1[l]) * (1.0 + sc1) + sh1
        k_l, v_l, a_l, u_l, q_l, r_l, hy_l, gate_l = split_cols(h @ w_in[l], COL_SIZES)
        hc = rmsnorm(ctx, g_norm1[l]) * (1.0 + mods_c[1]) + mods_c[0]
        if last:
            pc = split_cols(hc @ w_in[l][:, :N_STATE_COLS], COL_SIZES[:4])
        else:
            pc = split_cols(hc @ w_in[l], COL_SIZES)

        lf_c, lb_c = gla_decays(pc[2], gla_wa2[l], gla_ba[l])
        q_c = None if last else to_heads(pc[4], GLA_DK) * q_scale
        o_c, S_f, S_b = gla_bidir(to_heads(pc[0], GLA_DK), to_heads(pc[1], GLA_DV), lf_c, lb_c, zeros_S, zeros_S, q_c)
        lf, lb = gla_decays(a_l, gla_wa2[l], gla_ba[l])
        o_l, _, _ = gla_bidir(to_heads(k_l, GLA_DK), to_heads(v_l, GLA_DV), lf, lb, S_f, S_b,
                              to_heads(q_l, GLA_DK) * q_scale)
        y_gla = gla_readout(o_l, r_l, gla_gnorm[l])

        disc_f = s5_discretize(s5_a_re[l, 0], s5_a_im[l, 0], s5_log_dt[l, 0], s5_b_re[l], s5_b_im[l])
        disc_b = s5_discretize(s5_a_re[l, 1], s5_a_im[l, 1], s5_log_dt[l, 1], s5_b_re[l], s5_b_im[l])
        c_mat = lax.complex(s5_c_re[l].astype(F32), s5_c_im[l].astype(F32))
        ys_c, x_f, x_b = s5_bidir(to_groups(pc[3]), disc_f, disc_b, zeros_x, zeros_x, None if last else c_mat)
        ys_l, _, _ = s5_bidir(to_groups(u_l), disc_f, disc_b, x_f, x_b, c_mat)
        y_s5 = s5_readout(ys_l, u_l, s5_d[l], s5_w_glu[l], s5_b_glu[l])

        hy_p = (hy_w1[l], hy_b1[l], hy_w2[l], hy_b2[l], hy_w3[l], hy_freq1[l], hy_freq2[l], hy_decay[l])
        y_hy = hyena_mix(hy_l, hy_conv[l], hy_p, hy_bias[l])

        mix = merge_branches(y_hy, y_gla, y_s5, gate_l, w_br_hy[l], w_br_gla[l], w_br_s5[l], w_out[l])
        x = x + (gt1 * mix).astype(x.dtype)
        h2 = rmsnorm(x, g_norm2[l]) * (1.0 + sc2) + sh2
        x = x + (gt2 * swiglu(h2, w_ffn_in[l], w_ffn_out[l])).astype(x.dtype)

        if not last:
            yc_hy = hyena_mix(pc[6], hy_conv[l], hy_p, hy_bias[l])
            yc_gla = gla_readout(o_c, pc[5], gla_gnorm[l])
            yc_s5 = s5_readout(ys_c, pc[3], s5_d[l], s5_w_glu[l], s5_b_glu[l])
            mix_c = merge_branches(yc_hy, yc_gla, yc_s5, pc[7], w_br_hy[l], w_br_gla[l], w_br_s5[l], w_out[l])
            ctx = ctx + (mods_c[2] * mix_c).astype(ctx.dtype)
            hc2 = rmsnorm(ctx, g_norm2[l]) * (1.0 + mods_c[4]) + mods_c[3]
            ctx = ctx + (mods_c[5] * swiglu(hc2, w_ffn_in[l], w_ffn_out[l])).astype(ctx.dtype)
    return rmsnorm(x, g_final)


_drawn_inputs = setup_inputs


def setup_inputs(seed=0):
    import zlib

    import numpy as np

    out = dict(_drawn_inputs(seed))
    spreads = {}
    factors = {'ctx': 4.307,
     'c_ctx': 6.604,
     'g_norm1': 4.662,
     'g_norm2': 28.659,
     'hy_freq1': 7.275,
     'hy_freq2': 5.342,
     'gla_wa2': 3.276,
     'gla_ba': 64.0,
     'gla_gnorm': 64.0,
     's5_a_re': 64.0,
     's5_a_im': 55.64,
     's5_log_dt': 64.0,
     's5_b_re': 64.0,
     's5_b_im': 64.0,
     's5_c_re': 64.0,
     's5_c_im': 64.0,
     's5_w_glu': 59.127,
     's5_b_glu': 64.0,
     'g_final': 8.526,
     's5_d': 5.432,
     'w_br_s5': 5.077}
    for name, (base, spread) in spreads.items():
        noise = np.random.default_rng([zlib.crc32(name.encode()), seed]).standard_normal(out[name].shape)
        drawn = base * np.exp(spread * noise) if base else spread * noise
        out[name] = jnp.asarray(drawn.astype(out[name].dtype))
    for name, factor in factors.items():
        out[name] = (out[name] * factor).astype(out[name].dtype)
    return out
```

```python
import math
from contextlib import ExitStack

import concourse.bass as bass
import numpy as np
from concourse import mybir

P = 128


def constants():
    L = 512
    f32 = np.float32
    ident = np.eye(P, dtype=f32)
    swap = np.zeros((P, P), f32)
    for m in range(64):
        swap[m + 64, m] = 1.0
        swap[m, m + 64] = -1.0
    s = np.arange(P)[:, None]
    c = np.arange(P)[None, :]
    same = (s // 64) == (c // 64)
    mask_f = (same & (s <= c)).astype(f32)
    mask_b = (same & (s >= c)).astype(f32)
    restart = np.ones(768, f32)
    restart[::64] = 0.0
    steps = np.arange(96, dtype=f32)
    rows = np.concatenate([restart, steps])
    t = np.linspace(0.0, 1.0, L, dtype=f32)
    bands = np.linspace(1e-4, 15, 16, dtype=f32)
    ang = (f32(2.0 * math.pi / L) * np.arange(L, dtype=f32)[:, None]) * bands[None]
    z = np.concatenate([t[:, None], np.cos(ang), -np.sin(ang)], axis=-1).astype(f32)
    order = np.concatenate([np.arange(0, L, 2), np.arange(1, L, 2)])
    tneg = -t[order].reshape(4, P).T
    j = np.arange(L // 2)
    fwd, inv = [], []
    for p in range(2):
        w = 2.0 * np.pi * (j[None, :] + 0.5) * (2 * j[:, None] + p) / (2 * L)
        fwd += [np.cos(w), np.sin(w)]
        inv += [np.cos(w).T, np.sin(w).T]
    return {
        "sq": np.concatenate([ident, swap, mask_f, mask_b, tneg], axis=1).astype(f32),
        "rows": rows, "zT": np.ascontiguousarray(z.T),
        "dft": np.stack(fwd + inv).astype(f32),
    }


def hybrid_block(nc, I, C, out):
    fp32, fp32r, i32 = mybir.dt.float32, mybir.dt.float32r, mybir.dt.int32
    ALU = mybir.AluOpType
    ACT = mybir.ActivationFunctionType
    MUL, ADD, SUB = ALU.mult, ALU.add, ALU.subtract

    L, LC, D = I["x"].shape[1], I["ctx"].shape[1], I["x"].shape[2]
    LT = L + LC
    KD = D // P
    DF = I["w_ffn_out"].shape[1]
    NF = DF // P
    NFH = NF // 2
    EPS = 1e-6
    CH = 64
    NCH, NCC = LT // CH, LC // CH
    T8 = 8
    NS, NSC, NSL = LT // T8, LC // T8, L // T8
    NB, GB = 8, 4
    RS, HS, SLOT = 4, 2, 2048
    MAGIC = 12582912.0
    TWO_PI = 2.0 * math.pi
    C1 = 6.28125
    C2 = round((TWO_PI - C1) * 2**20) / 2**20
    C3 = TWO_PI - C1 - C2
    PI_IN = 3.1415925
    FB = "fb"

    K0, V0, A0, U0, Q0, R0, H0, G0 = 0, 256, 768, 800, 1312, 1568, 2080, 3616

    es = ExitStack()
    with es:
        def sem(name):
            return es.enter_context(nc.semaphore(name))

        psum = es.enter_context(nc.psum_tensor("psum", [P, 8, 512], fp32))
        PS = [psum[:, b, :] for b in range(8)]
        bank_full = [sem(f"bank_full{b}") for b in range(8)]
        bank_free = [sem(f"bank_free{b}") for b in range(8)]
        w_full = [sem(f"w_full{s}") for s in range(RS)]
        sems = {}

        def S(name):
            if name not in sems:
                sems[name] = sem(name)
            return sems[name]

        def v3(ap, a):
            return ap.rearrange("p (a b) -> p a b", a=a)

        WORDS = 53200
        base = (nc.sbuf_base + 31) // 32 * 32
        placed = [0]

        def at_words(at, words, dtype=fp32):
            placed[0] += 1
            return nc.alloc_sbuf_tensor_at(f"buf{placed[0]}_{at}", [P, words], dtype, offset=base + 4 * at)[:, :]

        def over(name, at, words):
            return nc.alloc_sbuf_tensor_at(name, [P, words], fp32r, offset=base + 4 * at)[:, :]

        class Region:
            def __init__(self, at, end=WORDS):
                self.at, self.end = at, end

            def take(self, words):
                a = self.at
                self.at += words
                assert self.at <= self.end, (self.at, self.end)
                return at_words(a, words)

        r = Region(0)
        ring = r.take(RS * SLOT)
        ring_lo = over("ring_lo", 0, RS * SLOT)
        ring_hi = over("ring_hi", r.at, HS * SLOT)
        r.take(HS * SLOT)
        hT_at = r.at
        hT = v3(r.take(KD * L), KD)
        hT_lo = v3(over("hT_lo", hT_at, KD * L), KD)
        hT_hi = v3(over("hT_hi", r.at, KD * L), KD)
        r.take(KD * L)
        sq = r.take(4 * P + 8)[:, 0:4 * P + 4]
        ident, swap = sq[:, 0:P], sq[:, P:2 * P]
        mask = {"f": sq[:, 2 * P:3 * P], "b": sq[:, 3 * P:4 * P]}
        tneg = sq[:, 4 * P:4 * P + 4]
        ones = r.take(P)
        rows = r.take(LT + NS)
        restart, steps = rows[:, 0:LT], rows[:, LT:LT + NS]
        cols = r.take(2 * P)
        small = r.take(160)
        csil = small[:, 0:16].rearrange("p (k v) -> p k v", v=2)
        modc = small[:, 16:48].rearrange("p (j v) -> p j v", v=2)
        A1 = small[:, 48:64].rearrange("p (v k) -> p v k", v=2)
        ssq, rstd = small[:, 64:72], small[:, 72:80]
        mod2 = small[:, 80:112].rearrange("p (j v) -> p j v", v=2)
        A2 = small[:, 112:120]
        ss2, rs2 = small[:, 120:124], small[:, 124:128]
        ssf, rsf = small[:, 128:132], small[:, 132:136]
        epsc, halfpi = small[:, 136:137], small[:, 137:138]
        F = r.at

        mT = v3(at_words(F, KD * L), KD)
        hcT = v3(at_words(F, KD * LC), KD)
        hc_lo = v3(over("hc_lo", F, KD * LC), KD)
        hc_hi = v3(over("hc_hi", F + KD * LC, KD * LC), KD)
        U_at = WORDS - 32 * NS
        U = v3(at_words(U_at, 32 * NS), 32)
        oT_at = U_at - 4 * L
        oT = v3(at_words(oT_at, 4 * L), 4)
        y_gla = oT
        par_at = oT_at - 1312
        r = Region(par_at, oT_at)
        mrow = [r.take(256)[0:2, :] for _ in range(2)]
        par = [r.take(64) for _ in range(12)]
        dI = r.take(32)[0:16, :]
        r = Region(F, F + KD * L)
        Bm = [v3(r.take(512), 32) for _ in range(2)]
        t9 = [r.take(576) for _ in range(3)]
        crow = [v3(r.take(512), 4) for _ in range(2)]
        arow = v3(r.take(256)[0:64, :], 2)

        r = Region(F + KD * L, par_at)
        g0 = r.at
        kT = v3(r.take(2 * LT), 2)
        qT = v3(r.take(2 * L), 2)
        vt = v3(r.take(6 * 512), 6)
        la = v3(r.take(2 * LT), 2)
        gtmp = v3(r.take(2 * LT), 2)
        kd = v3(r.take(2 * LT), 2)
        kdT = v3(r.take(6 * 256), 6)
        qd = v3(r.take(2 * L), 2)
        kn = v3(r.take(2 * L), 2)
        attm = [v3(r.take(512), 4) for _ in range(2)]
        sh_at = r.at
        Sh = r.take((NCH + 1) * 256).rearrange("p (n m e) -> p n m e", m=2, e=P)
        decay = r.take(2 * NCH).rearrange("p (m n) -> p m n", m=2)
        wa2z = r.take(512)[0:32, :].rearrange("p (d n) -> p d n", d=2)
        ztile = {"f": v3(oT.rearrange("p h n -> p (h n)")[:, 0:2 * LT], 2), "b": v3(r.take(2 * LT), 2)}
        r = Region(sh_at, sh_at + 3328)
        ustage = [r.take(LT).rearrange("p (s n) -> p s n", s=T8) for _ in range(2)]
        aT = r.take(LT)
        rS = v3(at_words(g0, 4 * L), 4)
        la_at = g0 + 2 * LT + 2 * L + 6 * 512
        osq = v3(at_words(la_at, 4 * L), 4)
        r = Region(g0, sh_at)
        x_in = v3(r.take(4 * D), 4)
        c_in = v3(r.take(2 * D), 2)
        vec = r.take(2 * P)
        cvec = r.take(P)[0:16, :]
        mrow8 = [r.take(256)[0:2, :] for _ in range(8)]
        sqd = r.take(D)

        r = Region(F + KD * L, par_at)
        sig = [r.take(L) for _ in range(2)]
        mtmp = r.take(L)
        hy_at = r.at
        x2, x1, vv = (v3(r.take(4 * L), 4) for _ in range(3))
        V9 = {d: r.take(GB * 9 * 16).rearrange("p (g t j) -> p g t j", g=GB, t=9) for d in FB}
        WT = r.take(GB * P).rearrange("p (g s i) -> p g s i", g=GB, s=T8)
        Wt = v3(r.take(GB * P), GB)
        Mt = v3(r.take(GB * P), GB)
        Kall = r.take(GB * 15 * 16).rearrange("p (g t j) -> p g t j", g=GB, t=15)
        cosT, sinT = ([v3(r.take(GB * NS), GB) for _ in range(2)] for _ in range(2))
        Xc = {d: [v3(r.take(GB * NSL), GB), v3(restart[:, k * GB * NSL:(k + 1) * GB * NSL], GB)]
              for k, d in enumerate(FB)}
        dSp, Zs, zin, ztmp = (v3(r.take(GB * NS), GB) for _ in range(4))
        zwork = at_words(r.at - 2 * GB * NS, 2 * GB * NS)
        ych = v3(r.take(16 * NSL), 16)
        Bb = {d: [v3(r.take(512), 32) for _ in range(2)] for d in FB}
        Cm = [v3(r.take(512), 32) for _ in range(2)]
        Lr, Li = (v3(r.take(9 * 64), 9) for _ in range(2))
        dtmp = r.take(GB * 16)[0:16, :]
        y_s5 = v3(at_words(U_at, 4 * L), 4)
        G5 = oT

        r = Region(hy_at + 12 * L, oT_at)
        hs, hd = x1, vv
        Rp, Qp = x1, vv
        vtok = v3(r.take(4 * L), 4)
        x1tok = v3(r.take(4 * L), 4)
        dft = [v3(r.take(512), 2) for _ in range(8)]
        k_at = r.at
        Gk, Hk = (v3(r.take(4 * L), 4) for _ in range(2))
        htmp = Gk[0:64, 2:4, :]
        w3 = Gk[0:64, 0:2, :]
        adec = Hk[:, 0:2, :]
        r = Region(oT_at, U_at)
        hb_, fexp, rnorm = (r.take(L) for _ in range(3))
        hid = r.take(L)[0:64, :]
        r = Region(U_at + 4 * L)
        zT = r.take(L)[0:33, :]
        brow = at_words(U_at + 5 * L, L)[0:1, :]
        hw1 = cols[0:33, 192:256]
        hw2 = rows[0:64, 0:64]
        y_hy = x2

        r = Region(hy_at + 4 * L)
        xr = v3(r.take(4 * D), 4)
        gt = [r.take(D) for _ in range(2)]
        gfin = r.take(D)
        mh_at = r.at
        mT_hi = v3(over("mT_hi", mh_at, KD * L), KD)
        xn2 = v3(r.take(4 * D), 4)
        mT_lo = v3(over("mT_lo", F, KD * L), KD)
        act_at = r.at
        actT = v3(r.take(NFH * L), NFH)
        act_lo = v3(over("act_lo", act_at, NFH * L), NFH)
        bgt = [at_words(act_at + k * D, D) for k in range(2)]
        crep = v3(at_words(act_at + 2 * D, D), KD)
        act_hi = v3(over("act_hi", F, NFH * L), NFH)
        assert F + NFH * L <= hy_at
        sA = [r.take(L) for _ in range(2)]
        xtmp = r.take(L)

        scr_u = nc.dram_tensor("scr_u", [4 * P, LT], fp32, kind="Internal").ap()
        scr_y = nc.dram_tensor("scr_y", [4 * P, L], fp32, kind="Internal").ap()
        w_in, w_mod = I["w_in"][0], I["w_mod"][0]

        STEPS, plan, place, cum, split_order = [], [], {}, [0] * RS, []

        def want(name, *parts, split=True):
            n, at, dmas, views = len(plan), 0, [], []
            s = (n % RS) * SLOT
            m = len(split_order)
            h = (m % HS) * SLOT
            for src in parts:
                k, w = src.shape[0] // P, src.shape[1]
                size = k * w
                dmas.append((v3(ring[:, s + at:s + at + size], k), src.rearrange("(k p) n -> p k n", p=P)))
                if split:
                    views.append((v3(ring_hi[:, h + at:h + at + size], k),
                                  v3(ring_lo[:, s + at:s + at + size], k)))
                else:
                    views.append(dmas[-1][0])
                at += size
            assert at <= SLOT
            cum[n % RS] += 16 * len(dmas)
            plan.append((name, dmas))
            if split:
                split_order.append(name)
            place[name] = (n % RS, cum[n % RS], views, at, m, len(plan) - 1)

        def block(w, c0, n=256):
            return w[:, c0:c0 + n]

        def step(*a):
            STEPS.append(a)

        def cols_slot(name, c0, n=256):
            want(name, block(w_in, c0, n))

        BR = ("w_br_hy", "w_br_gla", "w_br_s5")
        step("setup")

        def mod_steps(*which):
            for n, i in enumerate(which):
                want(f"mod{i}", block(w_mod, 256 * i), split=False)
                step("mod", i)
                if n:
                    step("modT", which[n - 1])
                if i == 5:
                    step("cols")
            step("modT", which[-1])

        mod_steps(*range(8))
        step("rms")
        step("hT")
        cols_slot("k", K0)
        step("chan", "k", ("k0", "k1"), True)
        cols_slot("v0", V0)
        step("vhalf", 0)
        cols_slot("v1", V0 + 256)
        step("vhalf", 1)
        cols_slot("a", A0, 128)
        step("chan", "a", ("a",), True)
        step("a_ev")
        step("z")
        cols_slot("q", Q0)
        step("chan", "q", ("q0", "q1"), False)
        step("k_ev")
        step("gla_log", 0)
        for i in range(2):
            cols_slot(f"u{i}", U0 + 256 * i)
            step("chan", f"u{i}", (f"u{2 * i}", f"u{2 * i + 1}"), True)
            step("u_ev", 2 * i)
            step("u_ev", 2 * i + 1)
            if i == 0:
                step("gla_exp", 0)
        step("u_load")
        step("s5_load")
        for n in range(2):
            if n:
                step("gla_log", n)
                mod_steps(12, 17)
                step("gla_exp", n)
            mod_steps(13 + n, 15 + n)
            step("gla_states", n)
            for b in range(4):
                step("gla_att", n, b)
        step("s5_turn")
        cols_slot("r0", R0)
        step("chan", "r0", ("r0", "r1"), False)
        step("gla_norm")
        step("s5_angles")
        step("r_ev", 0)
        cols_slot("r1", R0 + 256)
        step("chan", "r1", ("r2", "r3"), False)
        step("r_ev", 1)
        step("gla_out")
        step("s5_factors")
        for i in (18, 19):
            want(f"mod{i}", block(w_mod, 256 * i), split=False)
            step("mod", i)

        def merge_steps(b):
            for jp in range(4):
                for h in range(2):
                    def unit(jp=jp, h=h):
                        if h == 0:
                            want(f"gate{b}{jp}", block(w_in, G0 + D * b + 256 * jp))
                        step("merge_g", b, jp, h)
                        return ("gate_ev", b, 2 * jp + h)
                    yield unit

                    def unit(jp=jp, h=h):
                        if h == 0:
                            want(f"br{b}{jp}", block(I[BR[b]][0], 256 * jp), split=False)
                        step("merge_b", b, jp, h)
                        return ("merge_ev", b, 2 * jp + h)
                    yield unit

        def hy_steps():
            for i in range(6):
                for h in range(2):
                    def unit(i=i, h=h):
                        if h == 0:
                            cols_slot(f"hy{i}", H0 + 256 * i)
                        step("hy", i, h)
                        return ("hy_ev", 2 * i + h)
                    yield unit

        beside = []
        ms, hy = list(merge_steps(1)), list(hy_steps())
        early, ms = ms[:6], ms[6:]
        while ms or hy:
            beside += ms[:2] + hy[:2]
            hy, ms = hy[2:], ms[2:]
        late = []

        def one_beside(more=True):
            if late:
                step(*late.pop(0))
            if beside and more:
                late.append(beside.pop(0)())

        evs = [u() for u in early]
        step(*evs[0])
        step(*evs[2])
        step("s5_init")
        step("s5_gen", 0, 0)
        for e in (1, 3, 4, 5):
            step(*evs[e])
        step("modT", 18)
        step("modT", 19)
        step("s5_w", 0, 0)
        for b in range(NB):
            for n in range(2):
                m = 2 * b + n
                one_beside(n == 0)
                step("s5_ds", b, n)
                step("s5_sw", b, n)
                one_beside()
                if n == 1:
                    step("s5_v", b, n)
                if m + 1 < 2 * NB:
                    step("s5_gen", *divmod(m + 1, 2))
                step("s5_x", b, n)
                if n == 0:
                    if b:
                        step("s5_y", b - 1)
                    step("s5_v", b, n)
                if m + 1 < 2 * NB:
                    step("s5_w", *divmod(m + 1, 2))
                step("s5_k", b, n)
        one_beside()
        step("s5_y", NB - 1)
        while late or beside:
            one_beside()
        step("hy_tok")
        ms = list(merge_steps(2))
        evs = [ms[0](), ms[2]()]
        beside = [ms[1]] + ms[3:]
        want("glu", I["s5_w_glu"][0], split=False)
        step("s5_gelu")
        for e in evs:
            step(*e)
        step("glu")
        step("hy_hid")
        for cv in range(2):
            for q in range(2):
                step("filter", cv, q)
                one_beside()
            step("fnorm", cv)
            one_beside()
            for k in range(2):
                step("fspec", cv, k)
                one_beside(False)
            step("uspec", cv, 0)
            one_beside()
            one_beside()
            step("uspec", cv, 1)
            for _ in range(3):
                one_beside()
            step("yinv", cv)
            one_beside(False)
        while late or beside:
            one_beside()
            one_beside()
        beside = list(merge_steps(0))
        while late or beside:
            one_beside()
        step("mT_split")
        for i in (8, 9, 10, 11):
            want(f"mod{i}", block(w_mod, 256 * i), split=False)
            step("gt", i)
        for i in range(4):
            want(f"wo{i}", block(I["w_out"][0], 256 * i))
            step("wo", i)
        step("norm2")
        for i in (20, 21, 22, 23):
            want(f"mod{i}", block(w_mod, 256 * i), split=False)
            step("gt", i)
        step("A2")
        step("h2T")
        for hf in range(2):
            for j in range(hf * NFH, (hf + 1) * NFH):
                want(f"ffn{j}", block(I["w_ffn_in"][0], P * j, P), block(I["w_ffn_in"][0], DF + P * j, P))
                step("ffn", j)
                if j > hf * NFH:
                    step("act_split", j - 1)
            step("act_split", j)
            for q in range(2):
                step("down_open", hf, q)
                for k in range(0, NFH, 4):
                    n = min(4, NFH - k)
                    name = f"dn{hf}{q}_{k}"
                    want(name, I["w_ffn_out"][0][P * (hf * NFH + k):P * (hf * NFH + k + n), 512 * q:512 * (q + 1)])
                    step("down", hf, q, k, n)
                step("down_ev", hf, q)
        step("final")

        first_use, last_use = {}, {}
        for at, st in enumerate(STEPS):
            k = st[0]
            used = {"mod": lambda: [f"mod{st[1]}"], "gt": lambda: [f"mod{st[1]}"], "glu": lambda: ["glu"],
                    "merge_b": lambda: [f"br{st[1]}{st[2]}"], "chan": lambda: [st[1]], "vhalf": lambda: [f"v{st[1]}"],
                    "merge_g": lambda: [f"gate{st[1]}{st[2]}"], "hy": lambda: [f"hy{st[1]}"],
                    "wo": lambda: [f"wo{st[1]}"], "ffn": lambda: [f"ffn{st[1]}"],
                    "down": lambda: [f"dn{st[1]}{st[2]}_{st[3]}"]}.get(k, lambda: [])()
            for u in used:
                first_use.setdefault(u, at)
                last_use[u] = at
        ahead = {}
        for m, name in enumerate(split_order):
            at = first_use[split_order[m - 1]] if m else first_use[name] - 1
            p = place[name][5]
            at = max(at, first_use[plan[p - 2][0]])
            if m >= HS:
                at = max(at, last_use[split_order[m - HS]] + 1)
            assert at <= first_use[name], name
            ahead.setdefault(at, []).append(name)
        STEPS = [x for at, st in enumerate(STEPS)
                 for x in ([("split", n) for n in ahead.get(at, [])] + [st])]
        last_job = {}

        jobs = {}

        def full(eng, name):
            b, use = jobs[name]
            eng.wait_ge(bank_full[b], use + 1)
            return PS[b]

        def freed(name):
            return bank_free[jobs[name][0]]

        def evacuated(eng, name):
            b, use = jobs[name]
            eng.wait_ge(bank_free[b], use + 1)

        def released(eng, slot):
            job = last_job[slot]
            if isinstance(job, int):
                eng.wait_ge(S("dn_used"), job)
            else:
                full(eng, job)

        def seq(d):
            return list(range(NCH)) if d == "f" else list(range(NCC))[::-1] + list(range(NCC, NCH))[::-1]

        block_ = es.enter_context(nc.Block())

        @block_.tensor
        def _(pe):
            def open_job(name):
                n = len(jobs)
                b, use = n % 8, n // 8
                if use:
                    pe.wait_ge(bank_free[b], use)
                jobs[name] = (b, use)
                return PS[b]

            def close(ins, name):
                ins.then_inc(bank_full[jobs[name][0]], 1)

            def raw(name):
                s, c, views, _, _, _ = place[name]
                pe.wait_ge(w_full[s], c)
                return views

            def halves(name):
                _, _, views, _, m, _ = place[name]
                pe.wait_ge(S("w_lo"), m + 1)
                return views

            def product(o, pairs, start=True, stop=True):
                pairs = list(pairs)
                for n, (a, b) in enumerate(pairs):
                    ins = nc.tensor.matmul(o, a, b, start=start and n == 0, stop=stop and n == len(pairs) - 1)
                return ins

            def product3(o, fours, start=True, stop=True):
                return product(o, (pr for (ah, al, bh, bl) in fours
                                   for pr in ((ah, bh), (ah, bl), (al, bh))), start, stop)

            def setup():
                pe.wait_ge(S("consts"), 16)
                pe.wait_ge(S("c_rows"), 32)
                o = open_job("cT")
                close(nc.tensor.transpose(o[:, 0:16], cvec, ident[0:16, 0:16]), "cT")
                pe.wait_ge(S("csil"), 1)

            def cols_():
                pe.wait_ge(S("vec_rows"), 16 * 14)
                o = open_job("vec")
                nc.tensor.transpose(o[:, 0:P], vec[:, 0:P], ident)
                close(nc.tensor.transpose(o[:, P:2 * P], vec[:, P:2 * P], ident), "vec")

            def mod(i):
                w, = raw(f"mod{i}")
                name = f"mr{i}"
                o = open_job(name)
                close(product(o[0:2, 0:256], ((csil[:, k, :], w[:, k, :]) for k in range(KD))), name)
                last_job[f"mod{i}"] = name

            def mod_T(i):
                evacuated(pe, f"mr{i}")
                if i < 8:
                    name, at, row = "modA", 4 * i, mrow8[i]
                else:
                    name, at, row = f"mod{i}", 0, mrow[i % 2]
                o = open_job(name) if name not in jobs else PS[jobs[name][0]]
                for h in range(2):
                    ins = nc.tensor.transpose(o[:, at + 2 * h:at + 2 * h + 2], row[:, h * P:(h + 1) * P],
                                              ident[0:2, 0:2])
                if i >= 7:
                    close(ins, name)

            def gt_rows(i):
                w, = raw(f"mod{i}")
                pe.wait_ge(S("crep"), 1)
                name = f"gt{i}"
                o = open_job(name)
                close(product(o[:, 0:256], ((crep[:, k, :], w[:, k, :]) for k in range(KD))), name)
                last_job[f"mod{i}"] = name

            def h_T():
                pe.wait_ge(S("xn"), 6)
                for k in range(KD):
                    for tag, src, n in (("c", c_in, 2), ("x", x_in, 4)):
                        o = open_job(f"{tag}T{k}")
                        for t in range(n):
                            ins = nc.tensor.transpose(o[:, t * P:(t + 1) * P], src[:, t, k * P:(k + 1) * P], ident)
                        close(ins, f"{tag}T{k}")
                pe.wait_ge(S("h_split"), 2 * KD)

            def chan(slot, names, ctx):
                (wh, wl), = halves(slot)
                for h, name in enumerate(names):
                    c = slice(h * P, (h + 1) * P)
                    for tag, xh, xl, N in (("C", hc_hi, hc_lo, LC), ("L", hT_hi, hT_lo, L)):
                        if tag == "C" and not ctx:
                            continue
                        o = open_job(name + tag)
                        close(product3(o[:, 0:N], ((wh[:, k, c], wl[:, k, c], xh[:, k, :], xl[:, k, :])
                                                   for k in range(KD))), name + tag)
                last_job[slot] = name + tag

            def vhalf(i):
                (wh, wl), = halves(f"v{i}")
                for t in range(6):
                    name = f"v{t}{i}"
                    o = open_job(name)
                    xh, xl, c = (hc_hi, hc_lo, t * P) if t < 2 else (hT_hi, hT_lo, (t - 2) * P)
                    close(product3(o[:, 0:256], ((xh[:, k, c:c + P], xl[:, k, c:c + P], wh[:, k, :], wl[:, k, :])
                                                 for k in range(KD))), name)
                last_job[f"v{i}"] = name

            def z():
                pe.wait_ge(S("wa2"), 32)
                evacuated(pe, "aL")
                evacuated(pe, "aC")
                for n, d in enumerate(FB):
                    for m in range(2):
                        for tag, c, N in (("C", 0, LC), ("L", LC, L)):
                            name = f"z{d}{m}{tag}"
                            o = open_job(name)
                            close(nc.tensor.matmul(o[:, 0:N], wa2z[:, n, m * P:(m + 1) * P], aT[0:32, c:c + N],
                                                   start=True, stop=True), name)

            def gla_states(n):
                d = FB[n]
                pe.wait_ge(S("kd"), n + 1)
                for t in range(0, 6, 2):
                    o = open_job(f"kd{d}{t}")
                    for tt in range(2):
                        for m in range(2):
                            ins = nc.tensor.transpose(o[:, (2 * tt + m) * P:(2 * tt + m + 1) * P],
                                                      kd[:, m, (t + tt) * P:(t + tt + 1) * P], ident)
                    close(ins, f"kd{d}{t}")
                for t in range(6):
                    for i in range(2):
                        evacuated(pe, f"v{t}{i}")
                for t in range(0, 6, 2):
                    evacuated(pe, f"kd{d}{t}")
                for c in seq(d)[:-1]:
                    name = f"dS{d}{c}"
                    o = open_job(name)
                    lo = CH * (c % 2)
                    for m in range(2):
                        for hh in range(2):
                            h = 2 * m + hh
                            ins = nc.tensor.matmul(o[64 * hh:64 * hh + 64, m * P:(m + 1) * P],
                                                   kdT[lo:lo + 64, c // 2, h * 64:(h + 1) * 64],
                                                   vt[lo:lo + 64, c // 2, h * P:(h + 1) * P],
                                                   start=True, stop=True)
                    close(ins, name)

            def gla_att(n, b):
                d = FB[n]
                if b == 0:
                    pe.wait_ge(S("states"), n + 1)
                for u in range(2):
                    name = f"att{d}{b}{u}"
                    o = open_job(name)
                    lo = 64 * u
                    for m in range(2):
                        ins = nc.tensor.matmul(o[:, m * P:(m + 1) * P], kn[lo:lo + 64, m, b * P:(b + 1) * P],
                                               qd[lo:lo + 64, m, b * P:(b + 1) * P], start=True, stop=True)
                    close(ins, name)
                for u in range(2):
                    evacuated(pe, f"att{d}{b}{u}")
                    name = f"o{d}{b}{u}"
                    o = open_job(name)
                    lo = 64 * u
                    for m in range(2):
                        h = 2 * m + u
                        nc.tensor.matmul(o[:, m * P:(m + 1) * P], vt[:, 2 + b, h * P:(h + 1) * P],
                                         attm[b % 2][:, h, :], start=True, stop=False)
                        for c in range(2):
                            at = b * P + c * CH
                            ins = nc.tensor.matmul(o[:, m * P + c * CH:m * P + (c + 1) * CH],
                                                   Sh[lo:lo + 64, seq(d).index(NCC + 2 * b + c), m, :],
                                                   qd[lo:lo + 64, m, at:at + CH], start=False, stop=(c == 1))
                    close(ins, name)

            def gla_norm():
                pe.wait_ge(S("ones"), 1)
                pe.wait_ge(S("osq"), 1)
                for h in range(4):
                    name = f"om{h}"
                    o = open_job(name)
                    close(nc.tensor.matmul(o[:, :], ones, osq[:, h, :], start=True, stop=True), name)

            def s5_turn():
                pe.wait_ge(S("s5_load"), 16 * 14)
                o = open_job("s5a")
                for k in range(2):
                    ins = nc.tensor.transpose(o[:, 64 * k:64 * k + 64], arow[:, k, :], ident[0:64, 0:64])
                close(ins, "s5a")

            def s5_init():
                for k in range(2):
                    o = open_job(f"s5c{k}")
                    for c in range(4):
                        ins = nc.tensor.transpose(o[:, c * P:(c + 1) * P], crow[k][:, c, :], ident)
                    close(ins, f"s5c{k}")
                pe.wait_ge(S("U"), 16 * 8)

            def s5_w(b, n):
                m = 2 * b + n
                pe.wait_ge(S("WT"), m + 1)
                name = f"W{m}"
                o = open_job(name)
                for g in range(GB):
                    ins = nc.tensor.transpose(o[:, g * P:(g + 1) * P], WT[:, g, :, :].rearrange("p s i -> p (s i)"),
                                              ident)
                close(ins, name)

            def s5_ds(b, n):
                m = 2 * b + n
                evacuated(pe, f"W{m}")
                name = f"dS5{m}"
                o = open_job(name)
                for g in range(GB):
                    ins = nc.tensor.matmul(o[:, g * NS:(g + 1) * NS], Wt[:, g, :], U[:, GB * b + g, :],
                                           start=True, stop=True)
                close(ins, name)

            def s5_sw(b, n):
                m = 2 * b + n
                evacuated(pe, f"dS5{m}")
                name = f"sw{m}"
                o = open_job(name)
                close(nc.tensor.matmul(o[:, 0:GB * NS], swap, dSp.rearrange("p g n -> p (g n)"),
                                       start=True, stop=True), name)

            def s5_k(b, n):
                m, d = 2 * b + n, FB[n]
                pe.wait_ge(S("V9"), m + 1)
                name = f"K{m}"
                o = open_job(name)
                for g in range(GB):
                    ins = nc.tensor.matmul(o[0:16, g * P:(g + 1) * P], Bb[d][0][:, GB * b + g, :],
                                           V9[d][:, g, n:n + 8, :].rearrange("p t j -> p (t j)"),
                                           start=True, stop=True)
                close(ins, name)

            def s5_x(b, n):
                m = 2 * b + n
                pe.wait_ge(S("Zs"), m + 1)
                name = f"zw{m}"
                o = open_job(name)
                close(nc.tensor.matmul(o[:, 0:GB * NSL], swap, Zs[:, :, NSC - 1:NS - 1], start=True, stop=True),
                      name)

            def s5_y(b):
                pe.wait_ge(S("Xc"), 2 * b + 2)
                pe.wait_ge(S("Mt"), 16 * 8 * (b + 1))
                name = f"y5{b}"
                o = open_job(name)
                for g in range(GB):
                    oo = o[:, g * NSL:(g + 1) * NSL]
                    nc.tensor.matmul(oo, Mt[:, g, :], U[:, GB * b + g, NSC:NS], start=True, stop=False)
                    nc.tensor.matmul(oo, V9["f"][:, g, 1:9, :].rearrange("p t j -> p (t j)"), Xc["f"][b % 2][:, g, :],
                                     start=False, stop=False)
                    ins = nc.tensor.matmul(oo, V9["b"][:, g, 0:8, :].rearrange("p t j -> p (t j)"),
                                           Xc["b"][b % 2][:, g, :], start=False, stop=True)
                close(ins, name)

            def glu():
                w, = raw("glu")
                pe.wait_ge(S("G5"), 1)
                for m in range(4):
                    o = open_job(f"glu{m}")
                    close(product(o, ((w[:, k, m * P:(m + 1) * P], G5[:, k, :]) for k in range(4))), f"glu{m}")
                last_job["glu"] = "glu3"

            def merge_g(b, jp, h):
                (wh, wl), = halves(f"gate{b}{jp}")
                c = slice(h * P, (h + 1) * P)
                name = f"g{b}{2 * jp + h}"
                o = open_job(name)
                close(product3(o, ((wh[:, k, c], wl[:, k, c], hT_hi[:, k, :], hT_lo[:, k, :]) for k in range(KD))),
                      name)
                last_job[f"gate{b}{jp}"] = name

            def merge_b(b, jp, h):
                wb, = raw(f"br{b}{jp}")
                pe.wait_ge(S(f"branch{b}"), 1)
                c = slice(h * P, (h + 1) * P)
                name = f"b{b}{2 * jp + h}"
                o = open_job(name)
                y = (y_hy, y_gla, y_s5)[b]
                close(product(o, ((wb[:, k, c], y[:, k, :]) for k in range(4))), name)
                last_job[f"br{b}{jp}"] = name

            def hy(i, h):
                (wh, wl), = halves(f"hy{i}")
                c = slice(h * P, (h + 1) * P)
                name = f"hy{2 * i + h}L"
                o = open_job(name)
                close(product3(o, ((wh[:, k, c], wl[:, k, c], hT_hi[:, k, :], hT_lo[:, k, :]) for k in range(KD))),
                      name)
                last_job[f"hy{i}"] = name

            def tok(p, h):
                return slice(p + 256 * h, p + 256 * h + 255, 2)

            def hy_tok():
                pe.wait_ge(S("conv"), 1)
                for nm, src in (("v", vv), ("x1", x1)):
                    for t in range(4):
                        name = f"{nm}t{t}"
                        o = open_job(name)
                        for c in range(4):
                            ins = nc.tensor.transpose(o[:, c * P:(c + 1) * P], src[:, c, tok(t // 2, t % 2)], ident)
                        close(ins, name)

            def hy_hid():
                pe.wait_ge(S("hy_load"), 16 * 12)
                for k, (w, x) in enumerate(((hw1, zT), (hw2, hid))):
                    if k:
                        pe.wait_ge(S("hid"), 1)
                    o = open_job(f"hid{k}")
                    close(nc.tensor.matmul(o[0:64, :], w, x, start=True, stop=True), f"hid{k}")

            def filt(cv, q):
                pe.wait_ge(S("hid"), 2)
                pe.wait_ge(S("w3"), 32 * (cv + 1))
                for t in range(4):
                    name = f"f{cv}{q}{t}"
                    o = open_job(name)
                    close(nc.tensor.matmul(o, hid[:, tok(t // 2, t % 2)], w3[:, q, :], start=True, stop=True), name)

            def fnorm(cv):
                pe.wait_ge(S("hsq"), 8 * cv + 8)
                name = f"hn{cv}"
                o = open_job(name)
                close(product(o, ((ones, q[:, t, :]) for q in (Gk, Hk) for t in range(4))), name)

            def fspec(cv, p):
                pe.wait_ge(S("hn"), cv + 1)
                for jt in range(2):
                    for nm, tab, src in (("G", 2 * p, hs), ("H", 2 * p + 1, hd)):
                        name = f"{nm}{cv}{p}{jt}"
                        o = open_job(name)
                        close(product(o, ((dft[tab][:, h, jt * P:(jt + 1) * P], src[:, 2 * p + h, :])
                                          for h in range(2))), name)

            def uspec(cv, jt):
                if cv == 0:
                    for t in range(4):
                        evacuated(pe, f"vt{t}")
                else:
                    pe.wait_ge(S("ztok"), 1)
                for p in range(2):
                    for nm, tab in (("E", 2 * p), ("F", 2 * p + 1)):
                        name = f"{nm}{cv}{p}{jt}"
                        o = open_job(name)
                        close(product(o, ((dft[tab][:, h, jt * P:(jt + 1) * P], vtok[:, 2 * p + h, :])
                                          for h in range(2))), name)

            def yinv(cv):
                pe.wait_ge(S("Y"), 2 * cv + 2)
                for t in range(4):
                    name = f"y{cv}{t}"
                    o = open_job(name)
                    cut = slice(t * P, (t + 1) * P)
                    if cv == 0:
                        p, h = divmod(t, 2)
                        hc = slice(h * P, (h + 1) * P)
                        ins = product(o, ((dft[4 + 2 * p + s][:, jt, hc], (Rp, Qp)[s][:, 2 * p + jt, :])
                                          for s in range(2) for jt in range(2)))
                    else:
                        for p in range(2):
                            ins = product(o[:, 256 * p:256 * p + 256],
                                          (((Rp, Qp)[s][:, 2 * p + jt, cut], dft[4 + 2 * p + s][:, jt, :])
                                           for s in range(2) for jt in range(2)))
                    close(ins, name)

            def wo(i):
                (wh, wl), = halves(f"wo{i}")
                pe.wait_ge(S("mT"), KD)
                for t in range(4):
                    name = f"wo{i}{t}"
                    o = open_job(name)
                    c = slice(t * P, (t + 1) * P)
                    close(product3(o[:, 0:256], ((mT_hi[:, k, c], mT_lo[:, k, c], wh[:, k, :], wl[:, k, :])
                                                 for k in range(KD))), name)
                last_job[f"wo{i}"] = name

            def h2_T():
                pe.wait_ge(S("xn2"), 4)
                for k in range(KD):
                    name = f"x2T{k}"
                    o = open_job(name)
                    for t in range(4):
                        ins = nc.tensor.transpose(o[:, t * P:(t + 1) * P], xn2[:, t, k * P:(k + 1) * P], ident)
                    close(ins, name)
                pe.wait_ge(S("h_split"), 3 * KD)

            def ffn(j):
                views = halves(f"ffn{j}")
                for nm, (wh, wl) in zip(("fa", "fb"), views):
                    name = f"{nm}{j}"
                    o = open_job(name)
                    close(product3(o, ((wh[:, k, :], wl[:, k, :], hT_hi[:, k, :], hT_lo[:, k, :])
                                       for k in range(KD))), name)
                last_job[f"ffn{j}"] = f"fb{j}"

            used = [0]
            acc = [None]

            def down_open(hf, q):
                acc[0] = [open_job(f"d{hf}{q}{t}") for t in range(4)]

            def down(hf, q, k0, n):
                slot = f"dn{hf}{q}_{k0}"
                (wh, wl), = halves(slot)
                for i in range(n):
                    k = k0 + i
                    pe.wait_ge(S("act_lo"), hf * NFH + k + 1)
                    for t in range(4):
                        c = slice(t * P, (t + 1) * P)
                        ins = product3(acc[0][t], [(act_hi[:, k, c], act_lo[:, k, c], wh[:, i, :], wl[:, i, :])],
                                       start=(k == 0), stop=(k == NFH - 1))
                        if k == NFH - 1:
                            close(ins, f"d{hf}{q}{t}")
                if k0 + n < NFH:
                    ins.then_inc(S("dn_used"), 1)
                    used[0] += 1
                    last_job[slot] = used[0]
                else:
                    last_job[slot] = f"d{hf}{q}3"

            stages = dict(setup=setup, cols=cols_, mod=mod, modT=mod_T, gt=gt_rows, hT=h_T,
                          s5_turn=s5_turn, chan=chan, vhalf=vhalf, z=z,
                          gla_states=gla_states, gla_att=gla_att, gla_norm=gla_norm, s5_init=s5_init,
                          s5_w=s5_w, s5_ds=s5_ds, s5_sw=s5_sw, s5_k=s5_k, s5_x=s5_x, s5_y=s5_y,
                          glu=glu, merge_g=merge_g, merge_b=merge_b,
                          hy=hy, hy_tok=hy_tok, hy_hid=hy_hid, filter=filt, fnorm=fnorm, fspec=fspec,
                          uspec=uspec, yinv=yinv, wo=wo, h2T=h2_T, ffn=ffn, down_open=down_open, down=down)
            for kind, *args in STEPS:
                if kind in stages:
                    stages[kind](*args)

        @block_.sync
        def _(sp):
            sp.dma_start(sq, C["sq"]).then_inc(S("consts"), 16)
            for n, (name, dmas) in enumerate(plan):
                if n == RS:
                    sp.dma_start(rows, C["rows"].partition_broadcast(P)).then_inc(S("rows"), 16)
                if n >= RS:
                    released(sp, plan[n - RS][0])
                for dst, src in dmas:
                    sp.dma_start(dst, src).then_inc(w_full[n % RS], 16)

        @block_.gpsimd
        def _(pool):
            cnt = [0]

            def link(ins):
                cnt[0] += 1
                ins.then_inc(S("pool_chain"), 1)
                pool.wait_ge(S("pool_chain"), cnt[0])

            def setup():
                link(nc.gpsimd.memset(vec, 0.0))
                at = 0
                vloads = [(I["b_mod"][0], 48), (I["g_norm1"][0], 8), (I["g_norm2"][0], 8),
                          (None, 16)] + \
                         [(I["hy_conv"][0][j], 12) for j in range(3)] + \
                         [(I["gla_gnorm"][0], 1), (I["s5_d"][0], 4), (I["s5_b_glu"][0], 4)]
                for src, n in vloads:
                    if src is None:
                        at += n
                        continue
                    pool.dma_start(vec[at:at + n, 0:P], src.rearrange("(r n) -> r n", n=P)).then_inc(S("vec_rows"), 16)
                    at += n
                for k, nm in enumerate(("hy_b1", "hy_b2", "hy_freq1", "hy_freq2")):
                    pool.dma_start(vec[4 + k:5 + k, P:P + 64], I[nm]).then_inc(S("vec_rows"), 16)
                pool.dma_start(vec[0:4, P:2 * P], I["gla_ba"][0].rearrange("d (m n) -> (d m) n", n=P))\
                    .then_inc(S("vec_rows"), 16)
                nc.gpsimd.memset(ones, 1.0).then_inc(S("ones"), 1)
                link(nc.gpsimd.memset(wa2z, 0.0))
                for d in range(2):
                    pool.dma_start(wa2z[16 * d:16 * d + 16, d, :], I["gla_wa2"][0][d]).then_inc(S("wa2"), 16)

            def split(name):
                s, c, views, size, m, _ = place[name]
                h = (m % HS) * SLOT
                pool.wait_ge(w_full[s], c)
                pool.wait_ge(S("w_hi"), m + 1)
                nc.gpsimd.tensor_tensor(ring_lo[:, s * SLOT:s * SLOT + size], ring[:, s * SLOT:s * SLOT + size],
                                        ring_hi[:, h:h + size].bitcast(fp32), SUB).then_inc(S("w_lo"), 1)

            def act_split(j):
                k = j % NFH
                pool.wait_ge(S("act_hi"), j + 1)
                nc.gpsimd.tensor_tensor(act_lo[:, k, :], actT[:, k, :], act_hi[:, k, :].bitcast(fp32), SUB)\
                    .then_inc(S("act_lo"), 1)

            def s5_load():
                full(pool, "u3C")
                ld = S("s5_load")
                pool.dma_start(par[0], I["s5_log_dt"][0].rearrange("d g -> (d g)").partition_broadcast(P))\
                    .then_inc(ld, 16)
                for k in range(2):
                    src = (I["s5_a_re"], I["s5_a_im"])[k][0].rearrange("d g p -> (d g) p")
                    for h in range(2):
                        pool.dma_start(arow[:, k, 64 * h:64 * h + 64], src).then_inc(ld, 16)
                    c_re, c_im = (I[x][0].rearrange("(c g) i p -> (g i) c p", c=4) for x in ("s5_c_re", "s5_c_im"))
                    pool.dma_start(crow[k][:, :, 0:64], (c_re, c_im)[k]).then_inc(ld, 16)
                    pool.dma_start(crow[k][:, :, 64:128], (c_im, c_re)[k]).then_inc(ld, 16)
                    b_re, b_im = (I[x][0].rearrange("g p i -> p g i") for x in ("s5_b_re", "s5_b_im"))
                    pool.dma_start(Bm[k][0:64, :, :], (b_re, b_im)[k]).then_inc(ld, 16)
                    pool.dma_start(Bm[k][64:128, :, :], (b_im, b_re)[k]).then_inc(ld, 16)
                pool.dma_start(dI, I["s5_d"][0].rearrange("(g i) -> i g", i=16),
                               allow_slow_non_contiguous=True).then_inc(ld, 16)

            def hy_tok():
                full(pool, f"y5{NB - 1}")
                pool.wait_ge(S("s5_end"), 1)
                pool.wait_ge(S("Yd"), 16 * 16)
                hl = S("hy_load")
                for k in range(8):
                    pool.dma_start(dft[k], C["dft"][k].rearrange("(t p) n -> p t n", p=P)).then_inc(hl, 16)
                pool.dma_start(zT, C["zT"]).then_inc(hl, 16)
                pool.dma_start(hw1, I["hy_w1"][0]).then_inc(hl, 16)
                pool.dma_start(hw2, I["hy_w2"][0]).then_inc(hl, 16)
                pool.dma_start(brow, I["hy_bias"][0][0:1, :]).then_inc(hl, 16)
                load_filters(0)

            def load_filters(cv):
                pool.dma_start(w3, I["hy_w3"][0][:, 2 * L * cv:2 * L * (cv + 1)].rearrange("p (a n) -> p a n", a=2))\
                    .then_inc(S("w3"), 16)
                pool.dma_start(adec, I["hy_decay"][0][2 * L * cv:2 * L * (cv + 1)].rearrange("(a n) -> a n", a=2)
                               .partition_broadcast(P)).then_inc(S("w3"), 16)

            def yinv(cv):
                if cv == 0:
                    pool.wait_ge(S("Y"), 2)
                    load_filters(1)
                    pool.wait_ge(S("hn"), 1)
                    pool.dma_start(brow, I["hy_bias"][0][1:2, :]).then_inc(S("brow"), 16)
                else:
                    pool.wait_ge(S("branch0"), 1)
                    ld = S("p4_load")
                    pool.dma_start(xr, I["x"][0].rearrange("(t p) d -> p t d", p=P)).then_inc(ld, 16)
                    pool.dma_start(bgt[0], I["b_mod"][0][2 * D:3 * D].partition_broadcast(P)).then_inc(ld, 16)
                    pool.dma_start(bgt[1], I["b_mod"][0][5 * D:6 * D].partition_broadcast(P)).then_inc(ld, 16)
                    pool.dma_start(gfin, I["g_final"].partition_broadcast(P)).then_inc(ld, 16)

            def final():
                for t in range(4):
                    pool.wait_ge(S("out"), t + 1)
                    pool.dma_start(out[0, t * P:(t + 1) * P, :], xr[:, t, :]).then_inc(S("stored"), 16)
                pool.wait_ge(S("stored"), 64)

            stages = dict(setup=setup, split=split, act_split=act_split, s5_load=s5_load, hy_tok=hy_tok,
                          yinv=yinv, final=final)
            for kind, *args in STEPS:
                if kind in stages:
                    stages[kind](*args)

        @block_.scalar
        def _(act):
            cnt = [0]
            A = nc.scalar.activation

            def link(ins):
                cnt[0] += 1
                ins.then_inc(S("act_chain"), 1)
                act.wait_ge(S("act_chain"), cnt[0])

            def signal(name):
                act.sem_inc(S(name), 1)

            def setup():
                for k, nm in enumerate(("c", "c_ctx")):
                    act.dma_start(cvec[8 * k:8 * k + 8, :], (I["c"][0], I["c_ctx"])[k].rearrange("(r n) -> r n", n=P))\
                        .then_inc(S("c_rows"), 16)
                act.dma_start(x_in, I["x"][0].rearrange("(t p) d -> p t d", p=P)).then_inc(S("x_in"), 16)
                act.dma_start(c_in, I["ctx"][0].rearrange("(t p) d -> p t d", p=P)).then_inc(S("x_in"), 16)
                o = full(act, "cT")
                A(csil, o[:, 0:16].rearrange("p (v k) -> p k v", v=2), ACT.Silu).then_inc(freed("cT"), 1)
                evacuated(act, "cT")
                signal("csil")
                act.wait_ge(S("x_in"), 32)
                for t, xx in enumerate(rowsx):
                    link(A(sqd, xx, ACT.Square, accum_out=ssq[:, t:t + 1]))
                signal("ssq")

            rowsx = [x_in[:, t, :] for t in range(4)] + [c_in[:, t, :] for t in range(2)]

            def cols_():
                o = full(act, "vec")
                A(cols, o[:, 0:2 * P], ACT.Copy).then_inc(freed("vec"), 1)

            def rms():
                act.wait_ge(S("ms"), 1)
                link(A(rstd[:, 0:6], ssq[:, 0:6], ACT.Sqrt))
                signal("rms")
                act.wait_ge(S("rstd"), 1)
                for t, xx in enumerate(rowsx):
                    A(xx, xx, ACT.Copy, scale=rstd[:, t:t + 1]).then_inc(S("xn"), 1)

            def h_T():
                act.wait_ge(S("A1"), 1)
                for k in range(KD):
                    for v, tag, dst, N in ((1, "c", hcT, LC), (0, "x", hT, L)):
                        name = f"{tag}T{k}"
                        o = full(act, name)
                        A(dst[:, k, :], o[:, 0:N], ACT.Identity, scale=A1[:, v, k:k + 1], bias=modc[:, k, v:v + 1])\
                            .then_inc(freed(name), 1)

            def split(name):
                s, c, views, size, m, _ = place[name]
                h = (m % HS) * SLOT
                act.wait_ge(w_full[s], c)
                if m >= HS:
                    released(act, split_order[m - HS])
                A(ring_hi[:, h:h + size], ring[:, s * SLOT:s * SLOT + size], ACT.Copy).then_inc(S("w_hi"), 1)

            def vhalf(i):
                for t in range(6):
                    name = f"v{t}{i}"
                    o = full(act, name)
                    A(vt[:, t, 256 * i:256 * i + 256], o[:, 0:256], ACT.Copy).then_inc(freed(name), 1)

            def u_ev(c):
                act.wait_ge(S("ustage"), c + 1)
                act.dma_start(scr_u[c * P:(c + 1) * P, :], ustage[c % 2].rearrange("p s n -> p (s n)"))\
                    .then_inc(S(f"scr_u{c % 2}"), 16)

            def u_load():
                for k in range(2):
                    act.wait_ge(S(f"scr_u{k}"), 32)
                su = scr_u.rearrange("(g i) (s n) -> s i g n", i=16, s=T8)
                for s in range(T8):
                    act.dma_start(U[16 * s:16 * s + 16, :, :], su[s]).then_inc(S("U"), 16)

            def gla_log(n):
                act.wait_ge(S("zx"), n + 1)
                link(A(gtmp, gtmp, ACT.Abs))
                link(A(gtmp, gtmp, ACT.Exp, scale=-1.0))
                link(A(gtmp, gtmp, ACT.Ln, bias=1.0))
                signal("softplus")

            def gla_exp(n):
                act.wait_ge(S("cum"), n + 1)
                link(A(kd, kd, ACT.Exp, scale=1.0 / 16))
                last = 63 if n == 0 else 0
                link(A(decay, la.rearrange("p m (n c) -> p m n c", c=CH)[:, :, :, last], ACT.Exp, scale=1.0 / 16))
                link(A(qd, la[:, :, LC:LT], ACT.Exp, scale=1.0 / 16))
                link(A(kn, la[:, :, LC:LT], ACT.Exp, scale=-1.0 / 16))
                signal("gexp")

            def gla_states(n):
                for t in range(0, 6, 2):
                    name = f"kd{FB[n]}{t}"
                    o = full(act, name)
                    A(kdT[:, t:t + 2, :], v3(o, 2), ACT.Copy).then_inc(freed(name), 1)

            def gla_att(n, b):
                if n == 0:
                    for u in range(2):
                        name = f"of{b}{u}"
                        o = full(act, name)
                        A(oT[:, u::2, b * P:(b + 1) * P], v3(o[:, 0:2 * P], 2), ACT.Copy).then_inc(freed(name), 1)

            def r_ev(i):
                act.wait_ge(S("states"), 2)
                for h in (2 * i, 2 * i + 1):
                    o = full(act, f"r{h}L")
                    A(rS[:, h, :], o, ACT.Silu).then_inc(freed(f"r{h}L"), 1)

            def gla_norm():
                act.wait_ge(S("oT"), 1)
                A(osq, oT, ACT.Square).then_inc(S("osq"), 1)
                for h in range(4):
                    o = full(act, f"om{h}")
                    A(osq[:, h, :], o, ACT.Sqrt, scale=1.0 / P, bias=epsc).then_inc(freed(f"om{h}"), 1)

            def s5_turn():
                act.wait_ge(S("s5_load"), 16 * 14)
                link(A(par[0], par[0], ACT.Exp))
                signal("dt")

            def s5_angles():
                act.wait_ge(S("ang"), 1)
                link(A(t9[1], t9[1], ACT.Exp))
                link(A(t9[2], t9[0], ACT.Abs))
                link(A(t9[0], t9[0], ACT.Sin))
                link(A(t9[2], t9[2], ACT.Sin, scale=-1.0, bias=halfpi))
                signal("ang")

            def s5_gen(b, n):
                m = 2 * b + n
                c, s = cosT[m % 2], sinT[m % 2]
                act.wait_ge(S("turns"), m + 1)
                link(A(c, s, ACT.Abs))
                link(A(s, s, ACT.Sin, scale=2 * PI_IN))
                A(c, c, ACT.Sin, scale=-2 * PI_IN, bias=halfpi).then_inc(S("cs"), 1)

            def s5_w(b, n):
                name = f"W{2 * b + n}"
                o = full(act, name)
                A(Wt, v3(o, GB), ACT.Copy).then_inc(freed(name), 1)

            def s5_ds(b, n):
                m = 2 * b + n
                name = f"dS5{m}"
                o = v3(full(act, name)[:, 0:GB * NS], GB)
                if m:
                    act.wait_ge(S("Zs"), m)
                if n == 0:
                    A(dSp, o, ACT.Copy).then_inc(freed(name), 1)
                else:
                    A(dSp[:, :, 0:NSC], o[:, :, NSC - 1::-1], ACT.Copy)
                    A(dSp[:, :, NSC:NS], o[:, :, NS - 1:NSC - 1:-1], ACT.Copy).then_inc(freed(name), 1)

            def s5_k(b, n):
                if n == 0:
                    return
                act.wait_ge(S("Kall"), b + 1)
                if b:
                    full(act, f"y5{b - 1}")
                for s in range(T8):
                    act.dma_start(Mt[16 * s:16 * s + 16, :, :],
                                  Kall[0:16, :, 7 - s:15 - s, :].rearrange("p g t j -> p g (t j)"))\
                        .then_inc(S("Mt"), 16)

            def s5_y(b):
                name = f"y5{b}"
                o = full(act, name)
                if b == NB // 2:
                    act.wait_ge(S("Yd"), 16 * 8)
                at = GB * (b % 4)
                A(ych[:, at:at + GB, :], v3(o[:, 0:GB * NSL], GB), ACT.Copy).then_inc(freed(name), 1)
                if b % 4 == 3:
                    evacuated(act, name)
                    for bb in range(b - 3, b):
                        evacuated(act, f"y5{bb}")
                    sy = scr_y.rearrange("(g j) (t n) -> t j g n", j=16, t=T8)
                    for s in range(T8):
                        act.dma_start(sy[s][:, 4 * b - 12:4 * b + 4, :], ych[16 * s:16 * s + 16, :, :])\
                            .then_inc(S("Yd"), 16)

            def s5_gelu():
                act.wait_ge(S("Yd"), 16 * 16)
                full(act, f"y5{NB - 1}")
                full(act, f"b1{KD - 1}")
                act.dma_start(y_s5, scr_y.rearrange("(c p) n -> p c n", p=P)).then_inc(S("Yb"), 16)
                act.wait_ge(S("Yb"), 16)
                for c in range(4):
                    ins = A(G5[:, c, :].rearrange("p (n s) -> p s n", s=T8),
                            y_s5[:, c, :].rearrange("p (s n) -> p s n", s=T8), ACT.Gelu_apprx_tanh)
                ins.then_inc(S("G5"), 1)

            def glu():
                act.wait_ge(S("G5"), 1)
                for m in range(4):
                    o = full(act, f"glu{m}")
                    A(y_s5[:, m, :], o, ACT.Sigmoid, bias=cols[:, 121 + m:122 + m]).then_inc(freed(f"glu{m}"), 1)

            turn = [0]

            def gate_ev(b, j):
                n = turn[0]
                turn[0] += 1
                o = full(act, f"g{b}{j}")
                if n >= 2:
                    act.wait_ge(S("sig_used"), n - 1)
                A(sig[n % 2], o, ACT.Sigmoid).then_inc(freed(f"g{b}{j}"), 1)

            def hy_tok():
                act.wait_ge(S("s5_end"), 1)
                full(act, f"y5{NB - 1}")
                act.wait_ge(S("Yd"), 16 * 16)
                for nm, dst in (("v", vtok), ("x1", x1tok)):
                    for t in range(4):
                        o = full(act, f"{nm}t{t}")
                        A(dst[:, t, :], o, ACT.Copy).then_inc(freed(f"{nm}t{t}"), 1)

            def hy_hid():
                for k in range(2):
                    act.wait_ge(S("harg"), k + 1)
                    A(hid, htmp[:, 0, :], ACT.Sin).then_inc(S("hid"), 1)

            def filt(cv, q):
                if q == 0:
                    act.wait_ge(S("w3"), 32 * (cv + 1))
                    link(A(adec, adec, ACT.Abs))
                for t in range(4):
                    n = 8 * cv + 4 * q + t
                    if n:
                        act.wait_ge(S("fused"), n)
                    A(fexp, adec[:, q, :], ACT.Exp, scale=tneg[:, t:t + 1]).then_inc(S("fexp"), 1)

            def fnorm(cv):
                act.wait_ge(S("hsd"), cv + 1)
                for t in range(4):
                    A(Gk[:, t, :], hs[:, t, :], ACT.Square).then_inc(S("hsq"), 1)
                    A(Hk[:, t, :], hd[:, t, :], ACT.Square).then_inc(S("hsq"), 1)
                o = full(act, f"hn{cv}")
                A(rnorm, o, ACT.Sqrt, scale=0.5, bias=epsc).then_inc(freed(f"hn{cv}"), 1)

            def fspec(cv, p):
                for jt in range(2):
                    for nm, dst in (("G", Gk), ("H", Hk)):
                        name = f"{nm}{cv}{p}{jt}"
                        o = full(act, name)
                        A(dst[:, 2 * p + jt, :], o, ACT.Copy).then_inc(freed(name), 1)

            def norm2():
                full(act, "wo33")
                for t in range(4):
                    act.wait_ge(S("x2"), t + 1)
                    link(A(xn2[:, t, :], xr[:, t, :], ACT.Square, accum_out=ss2[:, t:t + 1]))
                    signal("ss2")
                    act.wait_ge(S("ms2"), t + 1)
                    link(A(rs2[:, t:t + 1], ss2[:, t:t + 1], ACT.Sqrt))
                    signal("sd2")
                    act.wait_ge(S("rs2"), t + 1)
                    A(xn2[:, t, :], xr[:, t, :], ACT.Copy, scale=rs2[:, t:t + 1]).then_inc(S("xn2"), 1)

            def h2_T():
                act.wait_ge(S("A2"), 1)
                for k in range(KD):
                    name = f"x2T{k}"
                    o = full(act, name)
                    A(hT[:, k, :], o, ACT.Identity, scale=A2[:, k:k + 1], bias=mod2[:, k, 0:1])\
                        .then_inc(freed(name), 1)

            def ffn(j):
                o = full(act, f"fa{j}")
                if j >= 2:
                    act.wait_ge(S("silu_used"), j - 1)
                A(sA[j % 2], o, ACT.Silu).then_inc(freed(f"fa{j}"), 1)

            def act_split(j):
                act.wait_ge(S("act_raw"), j + 1)
                if j == NFH:
                    full(act, "d013")
                A(act_hi[:, j % NFH, :], actT[:, j % NFH, :], ACT.Copy).then_inc(S("act_hi"), 1)

            def final():
                for t in range(4):
                    act.wait_ge(S("x3"), t + 1)
                    link(A(xn2[:, t, :], xr[:, t, :], ACT.Square, accum_out=ssf[:, t:t + 1]))
                    signal("ssf")
                    act.wait_ge(S("msf"), t + 1)
                    link(A(rsf[:, t:t + 1], ssf[:, t:t + 1], ACT.Sqrt))
                    signal("sdf")

            stages = dict(setup=setup, cols=cols_, rms=rms, hT=h_T, split=split, vhalf=vhalf, u_ev=u_ev, u_load=u_load,
                          gla_log=gla_log, gla_exp=gla_exp, gla_states=gla_states, gla_att=gla_att, r_ev=r_ev,
                          gla_norm=gla_norm, s5_turn=s5_turn, s5_angles=s5_angles, s5_gen=s5_gen, s5_w=s5_w, s5_ds=s5_ds, s5_k=s5_k,
                          s5_y=s5_y, s5_gelu=s5_gelu, glu=glu, gate_ev=gate_ev, hy_tok=hy_tok, hy_hid=hy_hid,
                          filter=filt, fnorm=fnorm, fspec=fspec, norm2=norm2, h2T=h2_T, ffn=ffn,
                          act_split=act_split, final=final)
            for kind, *args in STEPS:
                if kind in stages:
                    stages[kind](*args)

        @block_.vector
        def _(dve):
            V = nc.vector
            cnt = [0]

            def go(ins):
                cnt[0] += 1
                ins.then_inc(S("dve_chain"), 1)
                return cnt[0]

            def need(n):
                dve.wait_ge(S("dve_chain"), n)

            def link(ins):
                need(go(ins))

            def signal(name):
                dve.sem_inc(S(name), 1)

            def setup():
                link(V.memset(epsc, EPS))
                link(V.memset(halfpi, math.pi / 2))

            def rms():
                dve.wait_ge(S("ssq"), 1)
                link(V.tensor_scalar(ssq[:, 0:6], ssq[:, 0:6], 1.0 / D, EPS, MUL, ADD))
                signal("ms")
                dve.wait_ge(S("rms"), 1)
                link(V.reciprocal(rstd[:, 0:6], rstd[:, 0:6]))
                signal("rstd")

            last_T = {}

            def mod(i):
                if i >= 8 and i % 2 in last_T:
                    full(dve, last_T[i % 2])
                o = full(dve, f"mr{i}")
                V.tensor_copy(mrow8[i] if i < 8 else mrow[i % 2], o[0:2, 0:256]).then_inc(freed(f"mr{i}"), 1)
                if i >= 8:
                    last_T[i % 2] = f"mod{i}"

            def mod_T(i):
                if i < 7:
                    return
                evacuated(dve, "vec")
                name = "modA" if i == 7 else f"mod{i}"
                o = full(dve, name)
                n, c = (16, 0) if i == 7 else (2, 2 * i)
                dst = modc if i == 7 else mod2[:, 2 * (i - 12):2 * (i - 12) + 2, :]
                V.tensor_tensor(dst, o[:, 0:2 * n].rearrange("p (j v) -> p j v", v=2),
                                cols[:, c:c + n].unsqueeze(2).to_broadcast([P, n, 2]), ADD)\
                    .then_inc(freed(name), 1)

            def h_T():
                evacuated(dve, "modA")
                for v in range(2):
                    link(V.scalar_tensor_tensor(A1[:, v, :], modc[:, 8:16, v], 1.0, cols[:, 48:56], ADD, MUL))
                signal("A1")
                for k in range(KD):
                    for tag, x, hi, lo in (("c", hcT, hc_hi, hc_lo), ("x", hT, hT_hi, hT_lo)):
                        evacuated(dve, f"{tag}T{k}")
                        link(V.tensor_copy(hi[:, k, :], x[:, k, :]))
                        V.tensor_tensor(lo[:, k, :], x[:, k, :], hi[:, k, :].bitcast(fp32), SUB)\
                            .then_inc(S("h_split"), 1)

            def a_ev():
                for tag, c, N in (("C", 0, LC), ("L", LC, L)):
                    o = full(dve, f"a{tag}")
                    V.tensor_copy(aT[0:32, c:c + N], o[0:32, 0:N]).then_inc(freed(f"a{tag}"), 1)

            def chan(slot, names, ctx):
                if slot == "k":
                    for m in range(2):
                        for tag, c, N in (("C", 0, LC), ("L", LC, L)):
                            o = full(dve, f"k{m}{tag}")
                            V.tensor_copy(kT[:, m, c:c + N], o[:, 0:N]).then_inc(freed(f"k{m}{tag}"), 1)

            def z():
                for n, d in enumerate(FB):
                    for m in range(2):
                        for tag, c, N in (("C", 0, LC), ("L", LC, L)):
                            name = f"z{d}{m}{tag}"
                            o = full(dve, name)
                            V.tensor_scalar(ztile[d][:, m, c:c + N], o[:, 0:N],
                                            cols[:, P + 2 * n + m:P + 2 * n + m + 1], None, ADD)\
                                .then_inc(freed(name), 1)
                for d in FB:
                    for m in range(2):
                        for tag in "CL":
                            evacuated(dve, f"z{d}{m}{tag}")

            def k_ev():
                for h in range(2):
                    go(V.memset(attm[h], 0.0))
                for m in range(2):
                    o = full(dve, f"q{m}L")
                    V.tensor_copy(qT[:, m, :], o).then_inc(freed(f"q{m}L"), 1)

            def gla_log(n):
                d = FB[n]
                dve.wait_ge(S("rows"), 16)
                link(V.tensor_copy(gtmp, ztile[d]))
                signal("zx")
                if n:
                    for b in range(4):
                        for u in range(2):
                            evacuated(dve, f"of{b}{u}")
                    for h in range(2):
                        go(V.memset(attm[h], 0.0))
                link(V.tensor_scalar(la, ztile[d], 0.0, None, ALU.min))
                dve.wait_ge(S("softplus"), n + 1)
                link(V.tensor_tensor(gtmp, la, gtmp, SUB))
                for m in range(2):
                    if d == "f":
                        go(V.tensor_tensor_scan(la[:, m, :], restart, gtmp[:, m, :], 0.0, MUL, ADD))
                    else:
                        go(V.tensor_tensor_scan(la[:, m, ::-1], restart, gtmp[:, m, ::-1], 0.0, MUL, ADD))
                need(cnt[0])
                lac = la.rearrange("p m (n c) -> p m n c", c=CH)
                last = 63 if d == "f" else 0
                for m in range(2):
                    go(V.tensor_tensor(kd[:, m, :].rearrange("p (n c) -> p n c", c=CH),
                                       lac[:, m, :, last:last + 1].to_broadcast([P, NCH, CH]),
                                       lac[:, m, :, :], SUB))
                need(cnt[0])
                signal("cum")

            def gla_exp(n):
                dve.wait_ge(S("gexp"), n + 1)
                V.tensor_tensor(kd, kd, kT, MUL).then_inc(S("kd"), 1)
                link(V.scalar_tensor_tensor(qd, qd, 0.125, qT, MUL, MUL))
                link(V.tensor_tensor(kn, kn, kT[:, :, LC:LT], MUL))

            def u_ev(c):
                if c >= 2:
                    dve.wait_ge(S(f"scr_u{c % 2}"), 16 * (c // 2))
                for tag, n0, N in (("C", 0, NSC), ("L", NSC, NSL)):
                    name = f"u{c}{tag}"
                    o = full(dve, name)
                    V.tensor_copy(ustage[c % 2][:, :, n0:n0 + N],
                                  o[:, 0:N * T8].rearrange("p (n s) -> p s n", s=T8)).then_inc(freed(name), 1)
                for tag in "CL":
                    evacuated(dve, f"u{c}{tag}")
                signal("ustage")

            def gla_states(n):
                d = FB[n]
                if n == 0:
                    for k in range(2):
                        dve.wait_ge(S(f"scr_u{k}"), 32)
                    link(V.memset(Sh[:, 0, :, :], 0.0))
                for i, c in enumerate(seq(d)[:-1]):
                    name = f"dS{d}{c}"
                    o = full(dve, name)
                    for m in range(2):
                        ins = V.scalar_tensor_tensor(Sh[:, i + 1, m, :], Sh[:, i, m, :], decay[:, m, c:c + 1],
                                                     o[:, m * P:(m + 1) * P], MUL, ADD)
                        if m == 0:
                            go(ins)
                    ins.then_inc(freed(name), 1)
                    need(cnt[0])
                    evacuated(dve, name)
                signal("states")

            def gla_att(n, b):
                d = FB[n]
                for u in range(2):
                    name = f"att{d}{b}{u}"
                    o = full(dve, name)
                    V.copy_predicated(attm[b % 2][:, u::2, :],
                                      mask[d].bitcast(i32).unsqueeze(1).to_broadcast([P, 2, P]),
                                      v3(o[:, 0:2 * P], 2)).then_inc(freed(name), 1)
                if d == "b":
                    for u in range(2):
                        name = f"ob{b}{u}"
                        o = full(dve, name)
                        V.tensor_tensor(oT[:, u::2, b * P:(b + 1) * P], v3(o[:, 0:2 * P], 2),
                                        oT[:, u::2, b * P:(b + 1) * P], ADD).then_inc(freed(name), 1)
                    if b == 3:
                        for bb in range(4):
                            for u in range(2):
                                evacuated(dve, f"ob{bb}{u}")
                        signal("oT")

            def gla_out():
                for h in range(4):
                    evacuated(dve, f"om{h}")
                    evacuated(dve, f"r{h}L")
                    link(V.reciprocal(osq[:, h, :], osq[:, h, :]))
                    link(V.scalar_tensor_tensor(oT[:, h, :], oT[:, h, :], cols[:, 116:117], osq[:, h, :], MUL, MUL))
                    link(V.tensor_tensor(y_gla[:, h, :], oT[:, h, :], rS[:, h, :], MUL))
                signal("branch1")

            are, aim, lre, lim, fr, fi, den, psi = par[1:9]
            tmpa, tmpb, rho = par[9:12]

            def reduce_angle(x, k):
                link(V.tensor_scalar(k, x, 1.0 / TWO_PI, MAGIC, MUL, ADD))
                link(V.tensor_scalar(k, k, MAGIC, None, SUB))
                for c in (C1, C2, C3):
                    link(V.scalar_tensor_tensor(x, k, -c, x, MUL, ADD))
                link(V.tensor_scalar(x, x, PI_IN, -PI_IN, ALU.min, ALU.max))

            def s5_angles():
                o = full(dve, "s5a")
                link(V.tensor_scalar(are, o[:, 0:64], -1e-4, None, ALU.min))
                V.tensor_copy(aim, o[:, 64:128]).then_inc(freed("s5a"), 1)
                evacuated(dve, "s5a")
                dve.wait_ge(S("dt"), 1)
                link(V.tensor_tensor(lre, are, par[0], MUL))
                link(V.tensor_tensor(lim, aim, par[0], MUL))
                a9, m9, k9 = (v3(t, 9) for t in t9)
                tau = steps[:, 0:9].unsqueeze(2).to_broadcast([P, 9, 64])
                link(V.tensor_tensor(m9, lre.unsqueeze(1).to_broadcast([P, 9, 64]), tau, MUL))
                link(V.tensor_tensor(a9, lim.unsqueeze(1).to_broadcast([P, 9, 64]), tau, MUL))
                reduce_angle(t9[0], t9[2])
                link(V.tensor_scalar(psi, t9[0][:, 8 * 64:9 * 64], 1.0 / TWO_PI, None, MUL))
                signal("ang")

            def s5_factors():
                dve.wait_ge(S("ang"), 2)
                link(V.tensor_copy(rho, v3(t9[1], 9)[:, 8, :]))
                link(V.tensor_scalar(Bm[1][0:64, :, :], Bm[1][0:64, :, :], -1.0, None, MUL))
                link(V.tensor_tensor(tmpa, are, are, MUL))
                link(V.tensor_tensor(tmpb, aim, aim, MUL))
                link(V.tensor_tensor(den, tmpa, tmpb, ADD))
                link(V.reciprocal(den, den))
                link(V.tensor_tensor(lre, v3(t9[1], 9)[:, 1, :], v3(t9[2], 9)[:, 1, :], MUL))
                link(V.tensor_scalar(lre, lre, -1.0, None, ADD))
                link(V.tensor_tensor(lim, v3(t9[1], 9)[:, 1, :], v3(t9[0], 9)[:, 1, :], MUL))
                link(V.tensor_tensor(tmpa, lre, are, MUL))
                link(V.tensor_tensor(tmpb, lim, aim, MUL))
                link(V.tensor_tensor(tmpa, tmpa, tmpb, ADD))
                link(V.tensor_tensor(fr, tmpa, den, MUL))
                link(V.tensor_tensor(tmpa, lim, are, MUL))
                link(V.tensor_tensor(tmpb, lre, aim, MUL))
                link(V.tensor_tensor(tmpa, tmpa, tmpb, SUB))
                link(V.tensor_tensor(fi, tmpa, den, MUL))

            def s5_init():
                a9, m9, k9 = (v3(t, 9) for t in t9)
                go(V.tensor_tensor(Li, m9, a9, MUL))
                go(V.tensor_tensor(Lr, m9, k9, MUL))
                o = full(dve, "s5c0")
                c1 = Cm[0].rearrange("p g i -> p (g i)")
                c2 = Cm[1].rearrange("p g i -> p (g i)")
                link(V.tensor_copy(c1[0:64, :], o[0:64, :]))
                V.tensor_scalar(c1[64:128, :], o[64:128, :], -1.0, None, MUL).then_inc(freed("s5c0"), 1)
                o = full(dve, "s5c1")
                V.tensor_scalar(c2, o, -1.0, None, MUL).then_inc(freed("s5c1"), 1)
                evacuated(dve, "s5c0")
                evacuated(dve, "s5c1")
                g3 = [v3(x.rearrange("p s i -> p (s i)") if len(x.shape) == 3 else x, 32)
                      for x in (Wt, Mt)]
                for n, d in enumerate(FB):
                    f_r = fr[:, 32 * n:32 * n + 32].unsqueeze(2).to_broadcast([P, 32, 16])
                    f_i = fi[:, 32 * n:32 * n + 32].unsqueeze(2).to_broadcast([P, 32, 16])
                    go(V.tensor_tensor(Bb[d][0], Bm[0], f_r, MUL))
                    go(V.tensor_tensor(g3[0], Bm[1], f_i, MUL))
                    go(V.tensor_tensor(Bb[d][1], Bm[1], f_r, MUL))
                    link(V.tensor_tensor(g3[1], Bm[0], f_i, MUL))
                    go(V.tensor_tensor(Bb[d][0], Bb[d][0], g3[0], ADD))
                    link(V.tensor_tensor(Bb[d][1], Bb[d][1], g3[1], SUB))

            def powers(span, gs, shape):
                return (x[:, span, gs].rearrange("p t g -> p g t").unsqueeze(3).to_broadcast(shape) for x in (Lr, Li))

            def s5_gen(b, n):
                m, d = 2 * b + n, FB[n]
                gs = slice(32 * n + GB * b, 32 * n + GB * b + GB)
                gb = slice(GB * b, GB * b + GB)
                c, s = cosT[m % 2], sinT[m % 2]
                if m:
                    full(dve, f"W{m - 1}")
                    dve.wait_ge(S("Zs"), m)
                a = go(V.tensor_tensor(s, psi[:, gs].unsqueeze(2).to_broadcast([P, GB, NS]),
                                       steps[:, 0:NS].unsqueeze(1).to_broadcast([P, GB, NS]), MUL))
                shape = [P, GB, T8, 16]
                lr, li = powers(slice(7, None, -1) if d == "f" else slice(0, 8), gs, shape)
                b1, b2 = (Bb[d][k][:, gb, :].unsqueeze(2).to_broadcast(shape) for k in range(2))
                wtmp = zwork[:, 0:GB * P].rearrange("p (g s i) -> p g s i", g=GB, s=T8)
                go(V.tensor_tensor(WT, lr, b1, MUL))
                w = go(V.tensor_tensor(wtmp, li, b2, MUL))
                need(a)
                a = go(V.tensor_scalar(c, s, MAGIC, MAGIC, ADD, SUB))
                need(w)
                V.tensor_tensor(WT, WT, wtmp, ADD).then_inc(S("WT"), 1)
                need(a)
                V.tensor_tensor(s, s, c, SUB).then_inc(S("turns"), 1)

            def s5_v(b, n):
                d = FB[n]
                gs = slice(32 * n + GB * b, 32 * n + GB * b + GB)
                gb = slice(GB * b, GB * b + GB)
                if b:
                    full(dve, f"y5{b - 1}")
                dve.wait_ge(S("Zs"), 2 * b + n + 1)
                shape = [P, GB, 9, 16]
                lr, li = powers(slice(0, 9) if d == "f" else slice(8, None, -1), gs, shape)
                k1, k2 = (Cm[k][:, gb, :].unsqueeze(2).to_broadcast(shape) for k in range(2))
                vtmp = zwork[:, 0:GB * 144].rearrange("p (g t i) -> p g t i", g=GB, t=9)
                go(V.tensor_tensor(V9[d], lr, k1, MUL))
                link(V.tensor_tensor(vtmp, li, k2, MUL))
                V.tensor_tensor(V9[d], V9[d], vtmp, ADD).then_inc(S("V9"), 1)
                dve.wait_ge(S("V9"), 2 * b + n + 1)

            def s5_sw(b, n):
                m, d = 2 * b + n, FB[n]
                gs = slice(32 * n + GB * b, 32 * n + GB * b + GB)
                c, s = cosT[m % 2], sinT[m % 2]
                dve.wait_ge(S("cs"), m + 1)
                evacuated(dve, f"dS5{m}")
                go(V.tensor_tensor(zin, c, dSp, MUL))
                name = f"sw{m}"
                o = full(dve, name)
                V.tensor_tensor(ztmp, s, v3(o[:, 0:GB * NS], GB), MUL).then_inc(freed(name), 1)
                need(cnt[0])
                evacuated(dve, name)
                link(V.tensor_tensor(zin, zin, ztmp, ADD))
                for g in range(GB):
                    ins = V.tensor_tensor_scan(Zs[:, g, :], rho[:, gs][:, g:g + 1].to_broadcast([P, NS]),
                                               zin[:, g, :], 0.0, MUL, ADD)
                ins.then_inc(S("Zs"), 1)

            def s5_k(b, n):
                m, d = 2 * b + n, FB[n]
                name = f"K{m}"
                o = full(dve, name)[0:16, :].rearrange("p (g t j) -> p g t j", g=GB, t=8)
                if n == 0 and b:
                    dve.wait_ge(S("Mt"), 16 * 8 * b)
                if d == "f":
                    gb = slice(GB * b, GB * b + GB)
                    go(V.tensor_tensor(v3(dtmp, GB), ident[0:16, 0:16].unsqueeze(1).to_broadcast([16, GB, 16]),
                                       dI[:, gb].unsqueeze(2).to_broadcast([16, GB, 16]), MUL))
                    V.tensor_copy(Kall[0:16, :, 7:15, :], o).then_inc(freed(name), 1)
                    evacuated(dve, name)
                    need(cnt[0])
                    link(V.tensor_tensor(Kall[0:16, :, 7, :], Kall[0:16, :, 7, :], v3(dtmp, GB), ADD))
                else:
                    go(V.tensor_copy(Kall[0:16, :, 0:7, :], o[:, :, 0:7, :]))
                    V.tensor_tensor(Kall[0:16, :, 7, :], Kall[0:16, :, 7, :], o[:, :, 7, :], ADD)\
                        .then_inc(freed(name), 1)
                    evacuated(dve, name)
                    need(cnt[0])
                    signal("Kall")
                if m == 2 * NB - 1:
                    signal("s5_end")

            def s5_x(b, n):
                m, d = 2 * b + n, FB[n]
                c, s = cosT[m % 2], sinT[m % 2]
                lat = slice(NSC - 1, NS - 1)
                if m + 1 < 2 * NB:
                    dve.wait_ge(S("WT"), m + 2)
                dve.wait_ge(S("Zs"), m + 1)
                if b > 1:
                    full(dve, f"y5{b - 2}")
                go(V.tensor_tensor(zin[:, :, 0:NSL], c[:, :, lat], Zs[:, :, lat], MUL))
                name = f"zw{m}"
                o = full(dve, name)
                V.tensor_tensor(ztmp[:, :, 0:NSL], s[:, :, lat], v3(o[:, 0:GB * NSL], GB), MUL)\
                    .then_inc(freed(name), 1)
                need(cnt[0])
                evacuated(dve, name)
                xo = Xc[d][b % 2] if d == "f" else Xc[d][b % 2][:, :, ::-1]
                V.tensor_tensor(xo, zin[:, :, 0:NSL], ztmp[:, :, 0:NSL], SUB).then_inc(S("Xc"), 1)
                dve.wait_ge(S("Xc"), m + 1)

            def glu():
                for m in range(4):
                    evacuated(dve, f"glu{m}")
                    link(V.tensor_tensor(y_s5[:, m, :], y_s5[:, m, :], G5[:, m, :], MUL))
                signal("branch2")

            turn = [0]

            def merge_ev(b, j):
                n = turn[0]
                turn[0] += 1
                name = f"b{b}{j}"
                evacuated(dve, f"g{b}{j}")
                o = full(dve, name)
                dst = mT[:, j, :] if b == 1 else mtmp
                V.tensor_tensor(dst, o, sig[n % 2], MUL).then_inc(freed(name), 1)
                evacuated(dve, name)
                signal("sig_used")
                if b != 1:
                    link(V.tensor_tensor(mT[:, j, :], mT[:, j, :], mtmp, ADD))
                if b == 0:
                    link(V.tensor_copy(mT_hi[:, j, :], mT[:, j, :]))
                    V.tensor_tensor(mT_lo[:, j, :], mT[:, j, :], mT_hi[:, j, :].bitcast(fp32), SUB)\
                        .then_inc(S("mT"), 1)

            def hy_ev(c):
                name = f"hy{c}L"
                o = full(dve, name)
                dst = (x1, x2, vv)[c // 4][:, c % 4, :]
                w = [cols[:, 80 + 12 * j + c:81 + 12 * j + c] for j in range(3)]
                link(V.tensor_scalar(dst, o, w[1], None, MUL))
                link(V.scalar_tensor_tensor(dst[:, 1:L], o[:, 0:L - 1], w[0], dst[:, 1:L], MUL, ADD))
                V.scalar_tensor_tensor(dst[:, 0:L - 1], o[:, 1:L], w[2], dst[:, 0:L - 1], MUL, ADD)\
                    .then_inc(freed(name), 1)
                if c == 11:
                    for cc in range(12):
                        evacuated(dve, f"hy{cc}L")
                    signal("conv")

            def hy_hid():
                for k in range(2):
                    name = f"hid{k}"
                    o = full(dve, name)
                    V.tensor_scalar(htmp[:, 0, :], o[0:64, :], cols[0:64, P + 4 + k:P + 5 + k],
                                    cols[0:64, P + 6 + k:P + 7 + k], ADD, MUL).then_inc(freed(name), 1)
                    evacuated(dve, name)
                    reduce_angle(htmp[:, 0, :], htmp[:, 1, :])
                    signal("harg")
                    dve.wait_ge(S("hid"), k + 1)

            def filt(cv, q):
                if cv == 0 and q == 0:
                    for t in range(4):
                        evacuated(dve, f"x1t{t}")
                        evacuated(dve, f"vt{t}")
                for t in range(4):
                    name = f"f{cv}{q}{t}"
                    o = full(dve, name)
                    dve.wait_ge(S("fexp"), 8 * cv + 4 * q + t + 1)
                    dst = hb_ if q else hs[:, t, :]
                    V.tensor_tensor(dst, o, fexp, MUL).then_inc(freed(name), 1)
                    evacuated(dve, name)
                    signal("fused")
                    if q:
                        link(V.tensor_tensor(hd[:, t, :], hs[:, t, :], hb_, SUB))
                        link(V.tensor_tensor(hs[:, t, :], hs[:, t, :], hb_, ADD))
                if q:
                    link(V.tensor_copy(hd[0:1, 0, :], hs[0:1, 0, :]))
                    signal("hsd")

            def fnorm(cv):
                evacuated(dve, f"hn{cv}")
                link(V.reciprocal(rnorm, rnorm))
                for t in range(4):
                    for h_ in (hs, hd):
                        go(V.scalar_tensor_tensor(h_[:, t, :], h_[:, t, :], 2.0 / L, rnorm, MUL, MUL))
                if cv:
                    dve.wait_ge(S("brow"), 16)
                else:
                    dve.wait_ge(S("hy_load"), 16 * 12)
                need(cnt[0])
                V.scalar_tensor_tensor(hs[0:1, 0, :], brow, 2.0 / L, hs[0:1, 0, :], MUL, ADD).then_inc(S("hn"), 1)

            def uspec(cv, jt):
                if jt == 0:
                    for p in range(2):
                        for j in range(2):
                            for nm in "GH":
                                evacuated(dve, f"{nm}{cv}{p}{j}")
                bank = {(nm, p): full(dve, f"{nm}{cv}{p}{jt}") for nm in "EF" for p in range(2)}
                kk = {("G", p): Gk[:, 2 * p + jt, :] for p in range(2)}
                kk.update({("H", p): Hk[:, 2 * p + jt, :] for p in range(2)})
                tmp = (hb_, fexp)
                k = 0
                for r in range(2):
                    for dst, terms in ((Rp, (("E", "G", ADD), ("F", "H", SUB))), (Qp, (("E", "H", ADD), ("F", "G", ADD)))):
                        d_ = dst[:, 2 * r + jt, :]
                        first = True
                        for u_, k_, op in terms:
                            for p in range(2):
                                src, fac = bank[u_, p], kk[k_, (r - p) % 2]
                                if first:
                                    link(V.tensor_tensor(d_, src, fac, MUL))
                                    first = False
                                else:
                                    link(V.tensor_tensor(tmp[k % 2], src, fac, MUL))
                                    go(V.tensor_tensor(d_, d_, tmp[k % 2], op))
                                    k += 1
                                need(cnt[0] - (0 if first else 1))
                        need(cnt[0])
                for nm in "EF":
                    for p in range(2):
                        dve.sem_inc(freed(f"{nm}{cv}{p}{jt}"), 1)
                signal("Y")

            def yinv(cv):
                for t in range(4):
                    name = f"y{cv}{t}"
                    o = full(dve, name)
                    if cv == 0:
                        V.tensor_tensor(vtok[:, t, :], o, x1tok[:, t, :], MUL).then_inc(freed(name), 1)
                    else:
                        y = y_hy[:, t, :].rearrange("p (n q) -> p q n", q=2)
                        V.tensor_tensor(y, v3(o, 2), y, MUL).then_inc(freed(name), 1)
                for t in range(4):
                    evacuated(dve, f"y{cv}{t}")
                if cv == 0:
                    signal("ztok")
                else:
                    signal("branch0")
                    link(V.tensor_copy(crep, csil[:, :, 0:1].to_broadcast([P, KD, P])))
                    signal("crep")

            def gt_rows(i):
                k = 0 if i < 12 else 1
                c = 256 * (i - (8, 20)[k])
                if i == 8:
                    dve.wait_ge(S("p4_load"), 64)
                name = f"gt{i}"
                o = full(dve, name)
                V.tensor_tensor(gt[k][:, c:c + 256], o[:, 0:256], bgt[k][:, c:c + 256], ADD).then_inc(freed(name), 1)
                evacuated(dve, name)

            def make_A2():
                for i in range(12, 20):
                    evacuated(dve, f"mod{i}")
                link(V.scalar_tensor_tensor(A2, mod2[:, 8:16, 0], 1.0, cols[:, 56:64], ADD, MUL))
                signal("A2")

            def wo(i):
                for t in range(4):
                    name = f"wo{i}{t}"
                    o = full(dve, name)
                    c = slice(256 * i, 256 * i + 256)
                    V.tensor_tensor(xtmp[:, 0:256], o[:, 0:256], gt[0][:, c], MUL).then_inc(freed(name), 1)
                    evacuated(dve, name)
                    link(V.tensor_tensor(xr[:, t, c], xr[:, t, c], xtmp[:, 0:256], ADD))
                    if i == 3:
                        signal("x2")

            def norm2():
                for t in range(4):
                    dve.wait_ge(S("ss2"), t + 1)
                    link(V.tensor_scalar(ss2[:, t:t + 1], ss2[:, t:t + 1], 1.0 / D, EPS, MUL, ADD))
                    signal("ms2")
                    dve.wait_ge(S("sd2"), t + 1)
                    link(V.reciprocal(rs2[:, t:t + 1], rs2[:, t:t + 1]))
                    signal("rs2")

            def h2_T():
                for k in range(KD):
                    evacuated(dve, f"x2T{k}")
                    link(V.tensor_copy(hT_hi[:, k, :], hT[:, k, :]))
                    V.tensor_tensor(hT_lo[:, k, :], hT[:, k, :], hT_hi[:, k, :].bitcast(fp32), SUB)\
                        .then_inc(S("h_split"), 1)

            def ffn(j):
                o = full(dve, f"fb{j}")
                if j == NFH:
                    full(dve, "d013")
                evacuated(dve, f"fa{j}")
                V.tensor_tensor(actT[:, j % NFH, :], o, sA[j % 2], MUL).then_inc(freed(f"fb{j}"), 1)
                evacuated(dve, f"fb{j}")
                signal("silu_used")
                signal("act_raw")

            def down_ev(hf, q):
                for t in range(4):
                    name = f"d{hf}{q}{t}"
                    o = full(dve, name)
                    c = slice(512 * q, 512 * q + 512)
                    V.tensor_tensor(xtmp, o, gt[1][:, c], MUL).then_inc(freed(name), 1)
                    evacuated(dve, name)
                    link(V.tensor_tensor(xr[:, t, c], xr[:, t, c], xtmp, ADD))
                    if (hf, q) == (1, 1):
                        signal("x3")

            def final():
                for t in range(4):
                    dve.wait_ge(S("ssf"), t + 1)
                    link(V.tensor_scalar(ssf[:, t:t + 1], ssf[:, t:t + 1], 1.0 / D, EPS, MUL, ADD))
                    signal("msf")
                    dve.wait_ge(S("sdf"), t + 1)
                    link(V.reciprocal(rsf[:, t:t + 1], rsf[:, t:t + 1]))
                    link(V.scalar_tensor_tensor(xr[:, t, :], xr[:, t, :], rsf[:, t:t + 1], gfin, MUL, MUL))
                    signal("out")

            stages = dict(setup=setup, rms=rms, mod=mod, modT=mod_T, hT=h_T,
                          s5_angles=s5_angles, s5_factors=s5_factors, chan=chan, a_ev=a_ev, z=z, k_ev=k_ev, gla_log=gla_log,
                          gla_exp=gla_exp, u_ev=u_ev, gla_states=gla_states, gla_att=gla_att, gla_out=gla_out,
                          s5_init=s5_init, s5_gen=s5_gen, s5_v=s5_v, s5_sw=s5_sw, s5_k=s5_k, s5_x=s5_x, glu=glu,
                          merge_ev=merge_ev, hy_ev=hy_ev, hy_hid=hy_hid, filter=filt, fnorm=fnorm, uspec=uspec,
                          yinv=yinv, gt=gt_rows, A2=make_A2, wo=wo, norm2=norm2, h2T=h2_T, ffn=ffn,
                          down_ev=down_ev, final=final)
            for kind, *args in STEPS:
                if kind in stages:
                    stages[kind](*args)


def kernel(**inputs):
    import concourse.bacc as _bacc
    from concourse import mybir as _mybir
    from concourse.bass_utils import run_bass_kernel_spmd as _run

    nc = _bacc.Bacc("TRN2", target_bir_lowering=False, num_devices=1)
    arrays, ins, consts = {}, {}, {}
    for name, a in inputs.items():
        a = np.ascontiguousarray(a)
        arrays[f"in_{name}"] = a
        ins[name] = nc.dram_tensor(f"in_{name}", a.shape, _mybir.dt.from_np(a.dtype), kind="ExternalInput").ap()
    for name, a in constants().items():
        arrays[f"const_{name}"] = a
        consts[name] = nc.dram_tensor(f"const_{name}", a.shape, _mybir.dt.from_np(a.dtype),
                                      kind="ExternalInput").ap()
    out = nc.dram_tensor("out", (1, 512, 1024), _mybir.dt.float32, kind="ExternalOutput").ap()
    hybrid_block(nc, ins, consts, out)
    r = _run(nc, [arrays], core_ids=[0])
    return r.results[0]["out"]
```
